# Optimizing a Trainium2 kernel written in Bass

```python
import jax
import jax.numpy as jnp
from jax import lax
import numpy as np

D_MODEL = 1024
BATCH = 1
SEQ = 256
DEPTH = 2

D_A = D_MODEL // 2
A_HEAD_DIM = 128
A_HEADS = D_A // A_HEAD_DIM
A_CHUNK = 64
D_B = D_MODEL // 4
B_BLOCKS = 4
B_BLOCK_DIM = D_B // B_BLOCKS
CONV_WIDTH = 4
LRU_C = 8.0
D_C = D_MODEL // 4
C_GROUPS = 4
C_GROUP_DIM = D_C // C_GROUPS
C_CHUNK = 128

D_MIX = D_A + D_B + D_C
SPLIT_SIZES = (D_A, D_A, D_A, D_A, D_B, D_B, D_C, D_C)
D_IN = sum(SPLIT_SIZES)
D_FF = ((8 * D_MODEL // 3 + 127) // 128) * 128
EPS = 1e-6

kernel_name = 'hybrid_hgrn2_rglru_sgu_macaron'

def rmsnorm(x, gain):
    x32 = x.astype(jnp.float32)
    y = x32 * lax.rsqrt(jnp.mean(x32 * x32, axis=-1, keepdims=True) + EPS)
    return (y * gain.astype(jnp.float32)).astype(x.dtype)

def group_rmsnorm(x, gain, n_groups):
    shp = x.shape
    x32 = x.astype(jnp.float32).reshape(shp[:-1] + (n_groups, shp[-1] // n_groups))
    y = x32 * lax.rsqrt(jnp.mean(x32 * x32, axis=-1, keepdims=True) + EPS)
    return y.reshape(shp) * gain.astype(jnp.float32)

def swiglu(x, w_gate, w_up, w_down):
    return (jax.nn.silu(x @ w_gate) * (x @ w_up)) @ w_down

def hgrn2(q, f_logit, i, g, lower_bound, norm_gain):
    bsz, seq, _ = q.shape
    n_chunks = seq // A_CHUNK
    f32 = jnp.float32
    q = jax.nn.silu(q.astype(f32))
    lb = lower_bound.astype(f32)
    forget = lb + (1.0 - lb) * jax.nn.sigmoid(f_logit.astype(f32))
    k = 1.0 - forget
    log_f = jnp.log(forget)

    def to_chunks(t):
        return t.reshape(bsz, n_chunks, A_CHUNK, A_HEADS, A_HEAD_DIM).transpose(1, 0, 3, 2, 4)

    qc, kc, vc = to_chunks(q), to_chunks(k), to_chunks(i.astype(f32))
    bc = jnp.cumsum(to_chunks(log_f), axis=3)
    causal = jnp.tril(jnp.ones((A_CHUNK, A_CHUNK), bool))[:, :, None]

    def chunk_step(state, inp):
        q_t, k_t, v_t, b_t = inp
        diff = jnp.where(causal, b_t[:, :, :, None, :] - b_t[:, :, None, :, :], -jnp.inf)
        scores = jnp.einsum('bhtk,bhtsk,bhsk->bhts', q_t, jnp.exp(diff), k_t)
        out = (jnp.einsum('bhts,bhsv->bhtv', scores, v_t)
               + jnp.einsum('bhtk,bhkv->bhtv', q_t * jnp.exp(b_t), state))
        b_end = b_t[:, :, -1:, :]
        state = (jnp.exp(b_end[:, :, 0, :, None]) * state
                 + jnp.einsum('bhsk,bhsv->bhkv', k_t * jnp.exp(b_end - b_t), v_t))
        return state, out

    state0 = jnp.zeros((bsz, A_HEADS, A_HEAD_DIM, A_HEAD_DIM), f32)
    _, o = lax.scan(chunk_step, state0, (qc, kc, vc, bc))
    o = o.transpose(1, 0, 3, 2, 4).reshape(bsz, seq, D_A)
    o = group_rmsnorm(o, norm_gain, A_HEADS) * jax.nn.silu(g.astype(f32))
    return o.astype(g.dtype)

def rglru(xb, gate, conv_w, conv_b, w_a, b_a, w_x, b_x, lam, norm_gain):
    bsz, seq, _ = xb.shape
    f32 = jnp.float32
    xp = jnp.pad(xb, ((0, 0), (CONV_WIDTH - 1, 0), (0, 0)))
    xc = conv_b + xp[:, 0:seq] * conv_w[0]
    for tap in range(1, CONV_WIDTH):
        xc = xc + xp[:, tap:tap + seq] * conv_w[tap]
    xh = xc.reshape(bsz, seq, B_BLOCKS, B_BLOCK_DIM)
    r = jax.nn.sigmoid((jnp.einsum('blhi,hij->blhj', xh, w_a) + b_a).astype(f32)).reshape(bsz, seq, D_B)
    gate_in = jax.nn.sigmoid((jnp.einsum('blhi,hij->blhj', xh, w_x) + b_x).astype(f32)).reshape(bsz, seq, D_B)
    log_a = -LRU_C * r * jax.nn.softplus(-lam.astype(f32))
    a = jnp.exp(log_a)
    mult = jnp.sqrt(-jnp.expm1(2.0 * log_a))
    u = mult * gate_in * xc.astype(f32)

    def combine(left, right):
        return right[0] * left[0], right[0] * left[1] + right[1]

    _, h = lax.associative_scan(combine, (a, u), axis=1)
    y = h * jax.nn.gelu(gate.astype(f32))
    return group_rmsnorm(y, norm_gain, B_BLOCKS).astype(xb.dtype)

def chunked_sgu(u_in, v_in, w_s, b_s, norm_gain):
    bsz, seq, _ = u_in.shape
    n_chunks = seq // C_CHUNK
    f32 = jnp.float32
    u = jax.nn.gelu(u_in.astype(f32))
    v = jax.nn.gelu(v_in.astype(f32)).reshape(bsz, n_chunks, C_CHUNK, C_GROUPS, C_GROUP_DIM)
    mu = jnp.mean(v, axis=-1, keepdims=True)
    var = jnp.mean(jnp.square(v - mu), axis=-1, keepdims=True)
    v = (v - mu) * lax.rsqrt(var + EPS)
    w = w_s.astype(f32) * jnp.tril(jnp.ones((C_CHUNK, C_CHUNK), f32))
    z = jnp.einsum('gts,bnsgc->bntgc', w, v) + b_s.astype(f32).T[:, :, None]
    y = u * z.reshape(bsz, seq, D_C)
    return group_rmsnorm(y, norm_gain, C_GROUPS).astype(u_in.dtype)

def setup_inputs(seed: int = 0) -> dict:
    key = jax.random.key(seed)
    ks = jax.random.split(key, 32)
    f32 = jnp.float32

    def nrm(k, shape, scale):
        return jax.random.normal(k, shape, f32) * scale

    def gain(k, shape):
        return 1.0 + 0.05 * jax.random.normal(k, shape, f32)

    a0 = jax.random.uniform(ks[15], (DEPTH, D_B), f32, 0.9, 0.999)
    lam = jnp.log(a0) - jnp.log1p(-a0)
    return {
        'x': jax.random.normal(ks[0], (BATCH, SEQ, D_MODEL), f32),
        'ffn1_norm': gain(ks[1], (DEPTH, D_MODEL)),
        'ffn1_wg': nrm(ks[2], (DEPTH, D_MODEL, D_FF), D_MODEL ** -0.5),
        'ffn1_wu': nrm(ks[3], (DEPTH, D_MODEL, D_FF), D_MODEL ** -0.5),
        'ffn1_wd': nrm(ks[4], (DEPTH, D_FF, D_MODEL), D_FF ** -0.5),
        'mix_norm': gain(ks[5], (DEPTH, D_MODEL)),
        'w_in': nrm(ks[6], (DEPTH, D_MODEL, D_IN), D_MODEL ** -0.5),
        'hgrn_lb_logits': nrm(ks[7], (DEPTH, D_A), 0.5),
        'hgrn_norm': gain(ks[8], (DEPTH, D_A)),
        'conv_w': nrm(ks[9], (DEPTH, CONV_WIDTH, D_B), CONV_WIDTH ** -0.5),
        'conv_b': nrm(ks[10], (DEPTH, D_B), 0.02),
        'lru_wa': nrm(ks[11], (DEPTH, B_BLOCKS, B_BLOCK_DIM, B_BLOCK_DIM), B_BLOCK_DIM ** -0.5),
        'lru_ba': nrm(ks[12], (DEPTH, B_BLOCKS, B_BLOCK_DIM), 0.02),
        'lru_wx': nrm(ks[13], (DEPTH, B_BLOCKS, B_BLOCK_DIM, B_BLOCK_DIM), B_BLOCK_DIM ** -0.5),
        'lru_bx': nrm(ks[14], (DEPTH, B_BLOCKS, B_BLOCK_DIM), 0.02),
        'lru_lambda': lam,
        'lru_norm': gain(ks[16], (DEPTH, D_B)),
        'sgu_w': nrm(ks[17], (DEPTH, C_GROUPS, C_CHUNK, C_CHUNK), C_CHUNK ** -0.5),
        'sgu_b': gain(ks[18], (DEPTH, C_GROUPS, C_CHUNK)),
        'sgu_norm': gain(ks[19], (DEPTH, D_C)),
        'w_out': nrm(ks[20], (DEPTH, D_MIX, D_MODEL), D_MIX ** -0.5),
        'ffn2_norm': gain(ks[21], (DEPTH, D_MODEL)),
        'ffn2_wg': nrm(ks[22], (DEPTH, D_MODEL, D_FF), D_MODEL ** -0.5),
        'ffn2_wu': nrm(ks[23], (DEPTH, D_MODEL, D_FF), D_MODEL ** -0.5),
        'ffn2_wd': nrm(ks[24], (DEPTH, D_FF, D_MODEL), D_FF ** -0.5),
        'final_norm': gain(ks[25], (D_MODEL,)),
    }

def reference(x, ffn1_norm, ffn1_wg, ffn1_wu, ffn1_wd, mix_norm, w_in, hgrn_lb_logits, hgrn_norm,
              conv_w, conv_b, lru_wa, lru_ba, lru_wx, lru_bx, lru_lambda, lru_norm,
              sgu_w, sgu_b, sgu_norm, w_out, ffn2_norm, ffn2_wg, ffn2_wu, ffn2_wd, final_norm):
    lb_soft = jax.nn.softmax(hgrn_lb_logits.astype(jnp.float32), axis=0)
    lower_bounds = jnp.cumsum(lb_soft, axis=0) - lb_soft[0]
    split_points = [int(p) for p in np.cumsum(SPLIT_SIZES)[:-1]]
    h = x
    for layer in range(DEPTH):
        h = h + 0.5 * swiglu(rmsnorm(h, ffn1_norm[layer]), ffn1_wg[layer], ffn1_wu[layer], ffn1_wd[layer])
        z = rmsnorm(h, mix_norm[layer]) @ w_in[layer]
        q, f_logit, i, g, xb, gate, u, v = jnp.split(z, split_points, axis=-1)
        out_a = hgrn2(q, f_logit, i, g, lower_bounds[layer], hgrn_norm[layer])
        out_b = rglru(xb, gate, conv_w[layer], conv_b[layer], lru_wa[layer], lru_ba[layer],
                      lru_wx[layer], lru_bx[layer], lru_lambda[layer], lru_norm[layer])
        out_c = chunked_sgu(u, v, sgu_w[layer], sgu_b[layer], sgu_norm[layer])
        h = h + jnp.concatenate([out_a, out_b, out_c], axis=-1) @ w_out[layer]
        h = h + 0.5 * swiglu(rmsnorm(h, ffn2_norm[layer]), ffn2_wg[layer], ffn2_wu[layer], ffn2_wd[layer])
    return rmsnorm(h, final_norm)


_drawn_inputs = setup_inputs


def setup_inputs(seed=0):
    import zlib

    import numpy as np

    out = dict(_drawn_inputs(seed))
    spreads = {}
    factors = {'hgrn_lb_logits': 3.804, 'lru_ba': 8.0, 'lru_bx': 8.0, 'sgu_b': 4.723}
    for name, (base, spread) in spreads.items():
        noise = np.random.default_rng([zlib.crc32(name.encode()), seed]).standard_normal(out[name].shape)
        drawn = base * np.exp(spread * noise) if base else spread * noise
        out[name] = jnp.asarray(drawn.astype(out[name].dtype))
    for name, factor in factors.items():
        out[name] = (out[name] * factor).astype(out[name].dtype)
    return out
```

```python
import numpy as np

DEPTH, D, SEQ, DFF = 2, 1024, 256, 2816
P = 128
KT = D // P
TT = SEQ // P
CW = 256
CHUNK = KT * CW
FCH = DFF // CW
HEADS = 4
DA, DB, DC = 512, 256, 256
SUB = 64
EPS = 1e-6
N_IN, N_OUT = 12, 4
PER_LAYER = 2 * 3 * FCH + N_IN + N_OUT
IN_ORDER = (2, 3, 0, 1, 8, 9, 4, 5, 11, 10, 6, 7)
OUT_ORDER = (2, 3, 0, 1)
HALVES = (64, 32, 16, 8, 4, 2, 1)

C_N1, C_NM, C_N2, C_HN, C_CW, C_CB, C_BA, C_BX, C_LAM, C_GBC, C_LBL = 0, 8, 16, 24, 28, 36, 38, 40, 42, 44, 48
N_PAR = 52
C_LB, C_OML, C_C4, C_HBA, C_HBX, C_HHN = 52, 56, 60, 62, 64, 66
N_ALL = 70


def build(nc, x_in, wstream, params, gain_out, block_diag, sgu_wt, sgu_bias, identity, masks, causal, out):
    import concourse.bass as bass
    from concourse import mybir
    from contextlib import ExitStack

    F32, F32R, U8 = mybir.dt.float32, mybir.dt.float32r, mybir.dt.uint8
    ALU, ACT, AX = mybir.AluOpType, mybir.ActivationFunctionType, mybir.AxisListType
    ds = bass.ds

    with ExitStack() as ctx:
        def sb(name, shape, dt=F32):
            return ctx.enter_context(nc.sbuf_tensor(name, shape, dt))

        def sem(name):
            return ctx.enter_context(nc.semaphore(name))

        raw = [sb(f"raw{s}", [P, CHUNK]) for s in range(3)]
        whi = [sb(f"whi{s}", [P, CHUNK], F32R) for s in range(3)]
        wlo = [sb(f"wlo{s}", [P, CHUNK], F32R) for s in range(3)]
        x = sb("x", [P, KT, SEQ])
        xhi = sb("xhi", [P, KT, SEQ], F32R)
        xlo = sb("xlo", [P, KT, SEQ], F32R)
        yhi = sb("yhi", [P, KT, SEQ], F32R)
        ylo = sb("ylo", [P, KT, SEQ], F32R)
        xsq = sb("xsq", [P, KT, SEQ])
        rinv = sb("rinv", [P, SEQ])
        rinv_tok = sb("rinv_tok", [P, TT])
        tokvar = sb("tokvar", [P, TT])
        rinv_rows = sb("rinv_rows", [P, TT, P])
        par_all = sb("par_all", [P, DEPTH, N_ALL])
        par = sb("par", [P, N_ALL])
        gain_fin = sb("gain_fin", [P, KT])
        bd = sb("bd", [P, 4, P])
        wt = sb("wt", [P, 4, P])
        tri = sb("tri", [P, P])
        sbias = sb("sbias", [1, 4, P])
        ident = sb("ident", [P, P])
        mask = sb("mask", [P, len(HALVES) + 1, P], U8)
        ones_col = sb("ones_col", [P, 1])
        half_ones = sb("half_ones", [P, 2])
        ones_row = sb("ones_row", [1, 64])
        reset = sb("reset", [P, HEADS * SEQ])
        neg_half = sb("neg_half", [P, 16])
        ahi = sb("ahi", [P, 2, SEQ], F32R)
        alo = sb("alo", [P, 2, SEQ], F32R)
        fz = sb("fz", [P, HEADS, SEQ])
        kk = sb("kk", [P, HEADS, SEQ])
        qz = sb("qz", [P, HEADS, SEQ])
        qs = sb("qs", [P, HEADS, SEQ])
        qq = sb("qq", [P, HEADS, SEQ])
        bc = sb("bc", [P, HEADS, SEQ])
        dist = [sb(f"dist{i}", [P, HEADS, SEQ]) for i in range(2)]
        wqk = [sb(f"wqk{i}", [P, HEADS, SEQ]) for i in range(2)]
        scores = sb("scores", [P, HEADS * TT, P])
        cross = sb("cross", [P, HEADS, P])
        vals = sb("vals", [P, TT, DA])
        gz = fz
        osq = kk
        gate_z, u_z = qz[:, 0:2, :], qz[:, 2:4, :]
        stat_a = sb("stat_a", [P, TT * HEADS])
        xpad = sb("xpad", [P, 2, 3 + SEQ])
        xc = sb("xc", [P, 2, SEQ])
        rt = sb("rt", [P, 2, SEQ])
        gt = sb("gt", [P, 2, SEQ])
        th = sb("th", [P, 2, SEQ])
        dec = sb("dec", [P, 2, SEQ])
        lin = sb("lin", [P, 2, SEQ])
        v_z = sb("v_z", [P, TT, DC])
        v_stat = sb("v_stat", [P, 24])
        y_bc = bc
        ysq = qq
        dec_sq = xsq[:, 0:2, :]
        rows = xsq[:, 4:8, :].rearrange("p j (a c) -> p (j a) c", c=64)
        rows_a = xsq[:, 0:4, :].rearrange("p j (a c) -> p (j a) c", c=P)
        gsc, gact, up, act_f = rt, gt, th, dec
        stat_bc = sb("stat_bc", [P, 16])

        ps = ctx.enter_context(nc.psum_tensor("ps", [P, 8 * 512], F32))

        def bank(b, n=1):
            return ps[:, 512 * b:512 * (b + n)]

        acc = bank(0, 4).rearrange("p (m t) -> p m t", t=SEQ)
        zb = [bank(4).rearrange("p (m t) -> p m t", t=SEQ), bank(5).rearrange("p (m t) -> p m t", t=SEQ)]
        normsum = ps[:, 6 * 512:6 * 512 + TT]
        sum_bc = ps[:, 6 * 512 + 8:6 * 512 + 24]
        sum_a = ps[:, 6 * 512 + 24:6 * 512 + 32]
        rinv_ps = ps[:, 6 * 512 + 256:7 * 512]
        sc_ps = bank(0, 2).rearrange("p (a t) -> p a t", t=P)
        cross_ps = bank(7).rearrange("p (a t) -> p a t", t=P)
        gate_ps = bank(2, 2).rearrange("p (a m t) -> p a m t", a=2, t=SEQ)
        o_ps = bank(0, 2).rearrange("p (h t) -> p h t", t=SEQ)
        rbc_ps = bank(2, 2).rearrange("p (j t) -> p j t", t=SEQ)
        ra_ps = bank(4, 2).rearrange("p (h t) -> p h t", t=SEQ)
        z_ps = bank(7).rearrange("p (j t) -> p j t", t=SEQ)

        const_landed, x_landed, out_landed = sem("const_landed"), sem("x_landed"), sem("out_landed")
        setup_chain, v_part = sem("setup_chain"), sem("v_part")
        small_landed, wt_masked = sem("small_landed"), sem("wt_masked")
        landed = [sem(f"landed{s}") for s in range(3)]
        hi_ready = [sem(f"hi_ready{s}") for s in range(3)]
        lo_ready = [sem(f"lo_ready{s}") for s in range(3)]
        chunk_used = [sem(f"chunk_used{s}") for s in range(3)]
        setup_vec, setup_pool, setup_act = sem("setup_vec"), sem("setup_pool"), sem("setup_act")
        par_ready = sem("par_ready")
        x_ready = sem("x_ready")
        xhi_ready, xlo_ready = sem("xhi_ready"), sem("xlo_ready")
        xsq_ready = sem("xsq_ready")
        normsum_ready, var_ready, rtok_ready = sem("normsum_ready"), sem("var_ready"), sem("rtok_ready")
        rrows_ready, rps_ready, rinv_ready = sem("rrows_ready"), sem("rps_ready"), sem("rinv_ready")
        gsc_ready, gact_ready, up_ready = sem("gsc_ready"), sem("gact_ready"), sem("up_ready")
        actf_ready, ahi_ready, alo_ready = sem("actf_ready"), sem("ahi_ready"), sem("alo_ready")
        acc_done = sem("acc_done")
        z_free = [sem("z_free0"), sem("z_free1")]
        f_evac, f_sig, forget_ready, k_ready, clamp_ready = (
            sem("f_evac"), sem("f_sig"), sem("forget_ready"), sem("k_ready"), sem("clamp_ready"))
        logf_ready, b_ready = sem("logf_ready"), sem("b_ready")
        q_evac, q_sig, q_ready = sem("q_evac"), sem("q_sig"), sem("q_ready")
        dist_part = sem("dist_part")
        dist_ready, exp_ready = sem("dist_ready"), sem("exp_ready")
        wq_ready, wk_ready = sem("wq_ready"), sem("wk_ready")
        score_done, score_kept = sem("score_done"), sem("score_kept")
        cross_kept, keep_begun = sem("cross_kept"), sem("keep_begun")
        vals_ready = sem("vals_ready")
        xb_evac, conv_step, xc_ready = sem("xb_evac"), sem("conv_step"), sem("xc_ready")
        gates_done, rg_tanh, th_ready = sem("gates_done"), sem("rg_tanh"), sem("th_ready")
        dec_ready, dec2_ready, mult2_ready, mult_ready = (
            sem("dec_ready"), sem("dec2_ready"), sem("mult2_ready"), sem("mult_ready"))
        lin_part, lin_ready, h_ready, yb_ready = sem("lin_part"), sem("lin_ready"), sem("h_ready"), sem("yb_ready")
        gate_evac, gate_gelu, u_evac, u_gelu = sem("gate_evac"), sem("gate_gelu"), sem("u_evac"), sem("u_gelu")
        v_evac, v_gelu, v_mean, v_cent, v_sq, v_var, v_rstd, v_ready = (
            sem("v_evac"), sem("v_gelu"), sem("v_mean"), sem("v_cent"), sem("v_sq"), sem("v_var"),
            sem("v_rstd"), sem("v_ready"))
        z_done, yc_ready, ysq_ready, sumbc_done = sem("z_done"), sem("yc_ready"), sem("ysq_ready"), sem("sumbc_done")
        varbc, rstdbc, rowsbc, rbc_done, nbc_ready, yhbc, ylbc = (
            sem("varbc"), sem("rstdbc"), sem("rowsbc"), sem("rbc_done"), sem("nbc_ready"), sem("yhbc"), sem("ylbc"))
        g_evac, g_tanh, gs_ready = sem("g_evac"), sem("g_tanh"), sem("gs_ready")
        o_done, osq_ready, og_ready, suma_done = sem("o_done"), sem("osq_ready"), sem("og_ready"), sem("suma_done")
        vara, rstda, rowsa, ra_done, na_ready, yha, yla = (
            sem("vara"), sem("rstda"), sem("rowsa"), sem("ra_done"), sem("na_ready"), sem("yha"), sem("yla"))
        outt_ready = sem("outt_ready")

        USES = (2 * FCH + 6, 2 * FCH + 5, 2 * FCH + 5)

        def use_f(l, f, slot, i):
            first = 0 if f == 0 else (FCH + 6, FCH + 5, FCH + 5)[slot]
            return l * USES[slot] + (i + first)

        def use_in(l, n):
            return l * USES[n % 3] + (FCH + n // 3)

        def use_out(l, c):
            return l * USES[c % 3] + (FCH + 4 + c // 3)

        ROLES = ((0, 1, 2), (1, 2, 0))
        N_CONST = 5

        block = ctx.enter_context(nc.Block())

        @block.sync
        def _(sp):
            sp.dma_start(x[:], x_in).then_inc(x_landed, 16)

            def load(slot, use, chunk):
                sp.wait_ge(lo_ready[slot], use + 1)
                sp.dma_start(raw[slot][:], wstream[ds(chunk, 1)].rearrange("a p c -> p (a c)"))\
                    .then_inc(landed[slot], 16)

            def load_swiglu(l, f, first):
                g, u, d = ROLES[f]
                load(g, use_f(l, f, g, 0), first)
                load(u, use_f(l, f, u, 0), first + 1)
                with sp.Fori(0, FCH - 1) as i:
                    load(g, use_f(l, f, g, i + 1), first + i * 3 + 2)
                    load(u, use_f(l, f, u, i + 1), first + i * 3 + 3)
                    load(d, use_f(l, f, d, i), first + i * 3 + 4)
                load(d, use_f(l, f, d, FCH - 1), first + (3 * FCH - 1))

            with sp.Fori(0, DEPTH) as l:
                load_swiglu(l, 0, l * PER_LAYER)
                sp.wait_ge(x_ready, l * 12 + 1)
                for dst, src in ((bd, block_diag), (wt, sgu_wt), (sbias, sgu_bias)):
                    sp.dma_start(dst[:].rearrange("p a c -> p (a c)"),
                                 src[:, ds(l, 1), :].rearrange("p a c -> p (a c)")).then_inc(small_landed, 16)
                for n in range(N_IN):
                    load(n % 3, use_in(l, n), l * PER_LAYER + (3 * FCH + n))
                for c in range(N_OUT):
                    load(c % 3, use_out(l, c), l * PER_LAYER + (3 * FCH + N_IN + c))
                load_swiglu(l, 1, l * PER_LAYER + (3 * FCH + N_IN + N_OUT))
            for h in range(2):
                sp.wait_ge(outt_ready, h + 1)
                sp.dma_start(out[:, 4 * h:4 * h + 4, :], xsq[:, 4 * h:4 * h + 4, :]).then_inc(out_landed, 16)
            sp.wait_ge(out_landed, 32)

        @block.tensor
        def _(pe):
            mm = nc.tensor.matmul

            def mm3(dst, wh, wl, mh, ml, start, stop, shared=False):
                mm(dst, wh, mh, start=start, stop=False, skip_group_check=shared)
                mm(dst, wh, ml, start=False, stop=False, skip_group_check=shared)
                return mm(dst, wl, mh, start=False, stop=stop, skip_group_check=shared)

            def cols(slot, dst, m, wait_x=None):
                wh = whi[slot][:].rearrange("p (k c) -> p k c", k=KT)
                wl = wlo[slot][:].rearrange("p (k c) -> p k c", k=KT)
                for k in range(KT):
                    if wait_x is not None:
                        pe.wait_ge(xlo_ready, wait_x + (k + 1))
                    last = mm3(dst[:, m, :], wh[:, k, m * P:m * P + P], wl[:, k, m * P:m * P + P],
                               xhi[:, k, :], xlo[:, k, :], k == 0, k == KT - 1)
                return last

            def toks(slot, dst, t):
                wh = whi[slot][:].rearrange("p (k c) -> p k c", k=KT)
                wl = wlo[slot][:].rearrange("p (k c) -> p k c", k=KT)
                for k in range(KT):
                    last = mm3(dst[:, t, :], xhi[:, k, t * P:t * P + P], xlo[:, k, t * P:t * P + P],
                               wh[:, k, :], wl[:, k, :], k == 0, k == KT - 1)
                return last

            def sum_squares(norm):
                pe.wait_ge(xsq_ready, norm * 4 + 4)
                for t in range(TT):
                    for k in range(KT):
                        last = mm(normsum[:, t:t + 1], xsq[:, k, t * P:t * P + P], ones_col[:],
                                  start=(k == 0), stop=(k == KT - 1))
                last.then_inc(normsum_ready, 1)

            def spread_rinv(norm):
                pe.wait_ge(rrows_ready, norm + 1)
                for t in range(TT):
                    last = mm(rinv_ps[:, t * P:t * P + P], rinv_rows[:, t, :], ident[:], start=True, stop=True)
                last.then_inc(rps_ready, 1)

            def first_chunk(slot, use, norm, dst):
                pe.wait_ge(lo_ready[slot], use + 2)
                cols(slot, dst, 0, wait_x=norm * KT)
                sum_squares(norm)
                cols(slot, dst, 1).then_inc(chunk_used[slot], 1)
                spread_rinv(norm)

            def accumulate(slot, use, hi_in, lo_in, first, last):
                pe.wait_ge(lo_ready[slot], use + 2)
                wh = whi[slot][:].rearrange("p (k n) -> p k n", k=2)
                wl = wlo[slot][:].rearrange("p (k n) -> p k n", k=2)

                def one(k, m, stop):
                    return mm3(acc[:, m, :], wh[:, k, m * P:m * P + P], wl[:, k, m * P:m * P + P],
                               hi_in[:, k, :], lo_in[:, k, :], first and k == 0 and m % 2 == 0, stop, shared=True)

                if not last:
                    for k in range(2):
                        for m in range(KT):
                            ins = one(k, m, False)
                    ins.then_inc(chunk_used[slot], 1)
                else:
                    for b in range(4):
                        for m in (2 * b, 2 * b + 1):
                            for k in range(2):
                                ins = one(k, m, k == 1)
                        ins.then_inc(acc_done, 1)
                    mm(normsum[:, 0:1], ident[:], ones_col[:], start=True, stop=True).then_inc(chunk_used[slot], 1)

            def swiglu(l, f, norm):
                g, u, d = ROLES[f]
                done = l * (2 * FCH) + f * FCH
                first_chunk(g, use_f(l, f, g, 0), norm, zb[0])

                def up_chunk(i):
                    pe.wait_ge(lo_ready[u], use_f(l, f, u, i) + 2)
                    cols(u, zb[1], 0)
                    cols(u, zb[1], 1).then_inc(chunk_used[u], 1)

                def triple(i, first):
                    pe.wait_ge(lo_ready[g], use_f(l, f, g, i) + 2)
                    pe.wait_ge(gsc_ready, done + i)
                    cols(g, zb[0], 0)
                    cols(g, zb[0], 1).then_inc(chunk_used[g], 1)
                    pe.wait_ge(up_ready, done + i)
                    up_chunk(i)
                    pe.wait_ge(alo_ready, done + i)
                    accumulate(d, use_f(l, f, d, i - 1), ahi, alo, first, False)

                up_chunk(0)
                triple(1, True)
                with pe.Fori(2, FCH) as i:
                    triple(i, False)
                pe.wait_ge(alo_ready, done + FCH)
                accumulate(d, use_f(l, f, d, FCH - 1), ahi, alo, False, True)

            def score(l, j):
                if j == 0:
                    pe.wait_ge(k_ready, l + 1)
                    pe.wait_ge(q_ready, l * 2 + 2)
                    left, right = kk, qq
                else:
                    pe.wait_ge(wq_ready, l * 8 + j)
                    pe.wait_ge(wk_ready, l * 8 + j)
                    left = right = wqk[j % 2]
                if j == 1:
                    for h in range(HEADS):
                        last = mm(cross_ps[:, h, :], left[:, h, 0:P], right[:, h, P:2 * P], start=True, stop=True)
                else:
                    if j > 1:
                        pe.wait_ge(score_kept, l * 8 + (j - 1))
                    for h in range(HEADS):
                        for t in range(TT):
                            last = mm(sc_ps[:, h * TT + t, :], left[:, h, t * P:t * P + P],
                                      right[:, h, t * P:t * P + P], start=True, stop=True)
                last.then_inc(score_done, 1)

            def lru_gates(l):
                pe.wait_ge(small_landed, l * 48 + 48)
                pe.wait_ge(xc_ready, l * 2 + 2)
                for a in range(2):
                    for m in range(2):
                        last = mm(gate_ps[:, a, m, :], bd[:, 2 * a + m, :], xc[:, m, :], start=True, stop=True)
                last.then_inc(gates_done, 1)

            def sgu_mix(l):
                pe.wait_ge(v_ready, l + 1)
                pe.wait_ge(wt_masked, l + 1)
                pe.wait_ge(cross_kept, l + 1)
                for grp in range(4):
                    lo_p = 64 * (grp % 2)
                    for t in range(TT):
                        dst = z_ps[lo_p:lo_p + 64, grp // 2, t * P:t * P + P]
                        mm(dst, ones_row[:], sbias[:, grp, :], start=True, stop=False)
                        last = mm(dst, v_z[:, t, 64 * grp:64 * grp + 64], wt[:, grp, :], start=False, stop=True)
                last.then_inc(z_done, 1)

            def sums_bc(l):
                pe.wait_ge(ysq_ready, l + 1)
                for t in range(TT):
                    for j in range(4):
                        c = t * 8 + j * 2
                        last = mm(sum_bc[:, c:c + 2], ysq[:, j, t * P:t * P + P], half_ones[:], start=True, stop=True)
                last.then_inc(sumbc_done, 1)

            def spread_bc(l):
                pe.wait_ge(rowsbc, l + 1)
                r = xsq[:, 4:8, :].rearrange("p x (y c) -> p (x y) c", c=P)
                for j in range(4):
                    for t in range(TT):
                        last = mm(rbc_ps[:, j, t * P:t * P + P], r[:, 4 * t + j, :], ident[:], start=True, stop=True)
                last.then_inc(rbc_done, 1)

            def outputs_a(l):
                pe.wait_ge(vals_ready, l * 4 + 4)
                pe.wait_ge(score_kept, l * 8 + 8)
                for h in range(HEADS):
                    v0, v1 = vals[:, 0, h * P:h * P + P], vals[:, 1, h * P:h * P + P]
                    mm(o_ps[:, h, 0:P], v0, scores[:, h * TT, :], start=True, stop=True)
                    mm(o_ps[:, h, P:2 * P], v0, cross[:, h, :], start=True, stop=False)
                    last = mm(o_ps[:, h, P:2 * P], v1, scores[:, h * TT + 1, :], start=False, stop=True)
                last.then_inc(o_done, 1)

            def sums_a(l):
                pe.wait_ge(osq_ready, l + 1)
                for t in range(TT):
                    for h in range(HEADS):
                        c = t * HEADS + h
                        last = mm(sum_a[:, c:c + 1], osq[:, h, t * P:t * P + P], ones_col[:], start=True, stop=True)
                last.then_inc(suma_done, 1)

            def spread_a(l):
                pe.wait_ge(rowsa, l + 1)
                pe.wait_ge(z_free[0], l * 6 + 6)
                pe.wait_ge(z_free[1], l * 6 + 6)
                for h in range(HEADS):
                    for t in range(TT):
                        last = mm(ra_ps[:, h, t * P:t * P + P], rows_a[:, t * HEADS + h, :], ident[:], start=True, stop=True)
                last.then_inc(ra_done, 1)

            def mixer(l, norm):
                for n in range(N_IN):
                    slot, dst = n % 3, zb[n % 2]
                    if n == 0:
                        first_chunk(slot, use_in(l, n), norm, dst)
                    else:
                        pe.wait_ge(lo_ready[slot], use_in(l, n) + 2)
                        if n >= 2:
                            pe.wait_ge(z_free[n % 2], l * 6 + n // 2)
                        part = toks if n in (6, 7, 8) else cols
                        part(slot, dst, 0)
                        part(slot, dst, 1).then_inc(chunk_used[slot], 1)
                    if n >= 4:
                        score(l, n - 4)
                    if n == 5:
                        lru_gates(l)
                sgu_mix(l)
                score(l, 8)
                sums_bc(l)
                outputs_a(l)
                spread_bc(l)
                sums_a(l)
                pe.wait_ge(ylbc, l + 1)
                pe.wait_ge(og_ready, l + 1)
                accumulate(0, use_out(l, 0), yhi[:, 4:6, :], ylo[:, 4:6, :], True, False)
                spread_a(l)
                accumulate(1, use_out(l, 1), yhi[:, 6:8, :], ylo[:, 6:8, :], False, False)
                pe.wait_ge(yla, l + 1)
                accumulate(2, use_out(l, 2), yhi[:, 0:2, :], ylo[:, 0:2, :], False, False)
                accumulate(0, use_out(l, 3), yhi[:, 2:4, :], ylo[:, 2:4, :], False, True)

            for slot in range(3):
                pe.sem_inc(chunk_used[slot], 1)
            pe.wait_ge(const_landed, 16 * N_CONST)
            pe.wait_ge(setup_vec, 1)
            with pe.Fori(0, DEPTH) as l:
                pe.wait_ge(par_ready, l + 1)
                swiglu(l, 0, l * 3)
                mixer(l, l * 3 + 1)
                swiglu(l, 1, l * 3 + 2)
            sum_squares(3 * DEPTH)
            spread_rinv(3 * DEPTH)

        @block.scalar
        def _(act):
            A = nc.scalar.activation
            for dst, src in ((par_all[:, :, 0:N_PAR], params), (gain_fin[:], gain_out), (ident[:], identity),
                             (bc[:].rearrange("p h t -> p (h t)"), masks), (tri[:], causal)):
                act.dma_start(dst, src).then_inc(const_landed, 16)
            act.wait_ge(const_landed, 16 * N_CONST)
            lam = par_all[:, :, C_LAM:C_LAM + 2]
            tmp = v_stat[:, 0:4].rearrange("p (l c) -> p l c", l=DEPTH)
            tmp2 = v_stat[:, 4:8].rearrange("p (l c) -> p l c", l=DEPTH)
            A(tmp, lam, ACT.Abs).then_inc(setup_act, 1)
            act.wait_ge(setup_act, 1)
            A(tmp, tmp, ACT.Exp, scale=-1.0).then_inc(setup_act, 1)
            act.wait_ge(setup_act, 2)
            A(tmp, tmp, ACT.Ln, bias=1.0).then_inc(setup_act, 1)
            A(tmp2, lam, ACT.Relu, scale=-1.0).then_inc(setup_act, 1)
            act.wait_ge(setup_vec, 2)
            lbl = par_all[:, :, C_LBL:C_LBL + 4]
            A(lbl, lbl, ACT.Exp).then_inc(setup_act, 1)

            def hi(slot, use):
                act.wait_ge(landed[slot], use * 16 + 16)
                act.wait_ge(chunk_used[slot], use + 1)
                nc.scalar.copy(whi[slot][:], raw[slot][:]).then_inc(hi_ready[slot], 1)

            def split_x(col, m):
                A(xhi[:, m, :], x[:, m, :], ACT.Copy, scale=par[:, col + m:col + m + 1]).then_inc(xhi_ready, 1)

            def swiglu(l, f):
                g, u, d = ROLES[f]
                done = l * (2 * FCH) + f * FCH

                def silu(i):
                    act.wait_ge(gsc_ready, done + i + 1)
                    A(gact[:], gsc[:], ACT.Silu).then_inc(gact_ready, 1)

                def round_act(i):
                    act.wait_ge(actf_ready, done + i + 1)
                    act.wait_ge(chunk_used[d], use_f(l, f, d, i) + 1)
                    nc.scalar.copy(ahi[:], act_f[:]).then_inc(ahi_ready, 1)

                nc.scalar.preload_act_table(ACT.Silu)
                with act.Fori(0, FCH - 1) as i:
                    hi(g, use_f(l, f, g, i + 1))
                    silu(i)
                    hi(u, use_f(l, f, u, i + 1))
                    round_act(i)
                    hi(d, use_f(l, f, d, i))
                silu(FCH - 1)
                round_act(FCH - 1)
                hi(d, use_f(l, f, d, FCH - 1))

            def mixer(l):
                def exp_level(j):
                    act.wait_ge(dist_ready, l * 8 + j)
                    A(dist[j % 2][:], dist[j % 2][:], ACT.Exp).then_inc(exp_ready, 1)

                def vals_out(n):
                    act.wait_ge(chunk_used[n % 3], use_in(l, n) + 2)
                    c = (n - 6) * CW
                    A(vals[:, 0, c:c + CW], zb[n % 2][:, 0, :], ACT.Copy, scale=rinv_tok[:, 0:1]).then_inc(vals_ready, 1)
                    A(vals[:, 1, c:c + CW], zb[n % 2][:, 1, :], ACT.Copy, scale=rinv_tok[:, 1:2])\
                        .then_inc(vals_ready, 1)
                    act.wait_ge(vals_ready, l * 4 + (2 * (n - 6) + 2))
                    act.sem_inc(z_free[n % 2], 1)

                def hi_after(n):
                    m = n + 3
                    hi(m % 3, use_in(l, m) if m < N_IN else use_out(l, m - N_IN))

                for n in range(N_IN):
                    hi_after(n)
                    if n in (0, 1):
                        act.wait_ge(f_evac, l * 2 + n + 1)
                        A(fz[:, 2 * n:2 * n + 2, :], fz[:, 2 * n:2 * n + 2, :], ACT.Sigmoid).then_inc(f_sig, 1)
                    if n in (2, 3):
                        c = 2 * (n - 2)
                        act.wait_ge(q_evac, l * 2 + (n - 1))
                        A(qs[:, c:c + 2, :], qz[:, c:c + 2, :], ACT.Sigmoid).then_inc(q_sig, 1)
                    if n == 3:
                        act.wait_ge(clamp_ready, l + 1)
                        A(fz[:], fz[:], ACT.Ln).then_inc(logf_ready, 1)
                        exp_level(1)
                        exp_level(2)
                    if n == 5:
                        act.wait_ge(score_done, l * 9 + 2)
                        nc.scalar.copy(cross[:].rearrange("p a t -> p (a t)"), bank(7)).then_inc(cross_kept, 1)
                    if n in (6, 7):
                        vals_out(n)
                    if n == 6:
                        act.wait_ge(gates_done, l + 1)
                        for m in range(2):
                            A(rt[:, m, :], gate_ps[:, 0, m, :], ACT.Tanh, bias=par[:, C_HBA + m:C_HBA + m + 1],
                              scale=0.5).then_inc(rg_tanh, 1)
                            A(gt[:, m, :], gate_ps[:, 1, m, :], ACT.Tanh, bias=par[:, C_HBX + m:C_HBX + m + 1],
                              scale=0.5).then_inc(rg_tanh, 1)
                        act.wait_ge(rg_tanh, l * 4 + 4)
                        for m in range(2):
                            c4 = par[:, C_C4 + m:C_C4 + m + 1]
                            A(th[:, m, :], rt[:, m, :], ACT.Tanh, bias=c4, scale=c4).then_inc(th_ready, 1)
                            A(dec[:, m, :], rt[:, m, :], ACT.Exp, bias=c4, scale=c4).then_inc(dec_ready, 1)
                    if n == 8:
                        act.wait_ge(chunk_used[n % 3], use_in(l, n) + 2)
                        for t in range(TT):
                            A(v_z[:, t, :], zb[n % 2][:, t, :], ACT.Copy, scale=rinv_tok[:, t:t + 1])\
                                .then_inc(v_evac, 1)
                        act.wait_ge(v_evac, l * 2 + 2)
                        act.sem_inc(z_free[n % 2], 1)
                    if 4 <= n <= 9:
                        exp_level(n - 1)
                act.wait_ge(mult2_ready, l + 1)
                A(rt[:], th[:], ACT.Sqrt, scale=-0.25).then_inc(mult_ready, 1)
                act.wait_ge(v_evac, l * 2 + 2)
                A(v_z[:], v_z[:], ACT.Gelu_apprx_tanh).then_inc(v_gelu, 1)
                act.wait_ge(gate_evac, l + 1)
                A(gate_z, gate_z, ACT.Gelu_apprx_tanh).then_inc(gate_gelu, 1)
                act.wait_ge(u_evac, l + 1)
                A(u_z, u_z, ACT.Gelu_apprx_tanh).then_inc(u_gelu, 1)
                act.wait_ge(v_cent, l + 1)
                act.wait_ge(wq_ready, l * 8 + 8)
                nc.scalar.square(ysq[:, 0:2, :], v_z[:]).then_inc(v_sq, 1)
                act.wait_ge(g_evac, l * 2 + 2)
                A(qs[:], gz[:], ACT.Tanh, scale=0.5).then_inc(g_tanh, 1)
                act.wait_ge(o_done, l + 1)
                nc.scalar.square(osq[:], o_ps).then_inc(osq_ready, 1)
                act.wait_ge(nbc_ready, l * 4 + 4)
                nc.scalar.copy(yhi[:, 4:8, :], ysq[:]).then_inc(yhbc, 1)
                act.wait_ge(na_ready, l + 1)
                nc.scalar.copy(yhi[:, 0:4, :], osq[:]).then_inc(yha, 1)
                hi(0, use_out(l, 3))
                hi(1, use_f(l, 1, 1, 0))
                hi(2, use_f(l, 1, 2, 0))

            with act.Fori(0, DEPTH) as l:
                hi(1, use_f(l, 0, 1, 0))
                act.wait_ge(par_ready, l + 1)
                act.wait_ge(x_ready, l * 12 + 1)
                for m in range(KT):
                    split_x(C_N1, m)
                hi(0, use_f(l, 0, 0, 0))
                swiglu(l, 0)
                hi(0, use_in(l, 0))
                hi(1, use_in(l, 1))
                for m in range(KT):
                    if m % 2 == 0:
                        act.wait_ge(x_ready, l * 12 + (m // 2 + 2))
                    split_x(C_NM, m)
                hi(2, use_in(l, 2))
                mixer(l)
                for m in range(KT):
                    if m % 2 == 0:
                        act.wait_ge(x_ready, l * 12 + (m // 2 + 6))
                    split_x(C_N2, m)
                swiglu(l, 1)

        @block.gpsimd
        def _(pool):
            G = nc.gpsimd

            def squares(norm, updates):
                for b in range(4):
                    pool.wait_ge(x_ready, updates + (b + 2))
                    G.tensor_tensor(xsq[:, 2 * b:2 * b + 2, :], x[:, 2 * b:2 * b + 2, :], x[:, 2 * b:2 * b + 2, :],
                                    ALU.mult).then_inc(xsq_ready, 1)
                rsqrt_tok(norm)

            def rsqrt_tok(norm):
                pool.wait_ge(var_ready, norm + 1)
                G.tensor_tensor(rinv_tok[:], tokvar[:], neg_half[:, 0:TT], ALU.pow).then_inc(rtok_ready, 1)

            def distances(l, j):
                if j > 2:
                    pool.wait_ge(wq_ready, l * 8 + (j - 2))
                    pool.wait_ge(wk_ready, l * 8 + (j - 2))
                h = (128,) + HALVES
                h = h[j - 1]
                buf = dist[j % 2]
                if h == 128:
                    b = bc[:].rearrange("p h (c s) -> p h c s", s=SUB)
                    o = buf[:].rearrange("p h (c s) -> p h c s", s=SUB)

                    def end(c):
                        return b[:, :, c, SUB - 1:SUB].to_broadcast([P, HEADS, SUB])
                    G.tensor_tensor(o[:, :, 0, :], end(0), b[:, :, 0, :], ALU.subtract).then_inc(dist_part, 1)
                    G.tensor_tensor(o[:, :, 1, :], end(1), b[:, :, 1, :], ALU.subtract)
                    G.tensor_copy(o[:, :, 2, :], b[:, :, 2, :])
                    pool.wait_ge(dist_part, l + 1)
                    G.tensor_tensor(o[:, :, 0, :], o[:, :, 0, :], end(1), ALU.add)
                    G.tensor_tensor(o[:, :, 3, :], b[:, :, 3, :], end(2), ALU.add).then_inc(dist_ready, 1)
                    return
                b = bc[:].rearrange("p h (n two s) -> p (h n) two s", two=2, s=h)
                o = buf[:].rearrange("p h (n two s) -> p (h n) two s", two=2, s=h)
                end = b[:, :, 0, h - 1:h].to_broadcast([P, HEADS * SEQ // (2 * h), h])
                G.tensor_tensor(o[:, :, 0, :], end, b[:, :, 0, :], ALU.subtract)
                if h == SUB:
                    G.tensor_copy(o[:, :, 1, :], b[:, :, 1, :]).then_inc(dist_ready, 1)
                else:
                    G.tensor_tensor(o[:, :, 1, :], b[:, :, 1, :], end, ALU.subtract).then_inc(dist_ready, 1)

            def weigh_keys(l, j):
                h = ((128,) + HALVES)[j - 1]
                pool.wait_ge(exp_ready, l * 8 + j)
                if j > 2:
                    pool.wait_ge(score_done, l * 9 + (j - 1))
                sel = "p h (n two s) -> p (h n) two s"
                o, e, k = (t[:].rearrange(sel, two=2, s=h)[:, :, 0, :] for t in (wqk[j % 2], dist[j % 2], kk))
                G.tensor_tensor(o, e, k, ALU.mult).then_inc(wk_ready, 1)

            def mixer(l):
                for n in range(2):
                    pool.wait_ge(q_sig, l * 2 + n + 1)
                    G.tensor_tensor(qq[:, 2 * n:2 * n + 2, :], qz[:, 2 * n:2 * n + 2, :], qs[:, 2 * n:2 * n + 2, :],
                                    ALU.mult).then_inc(q_ready, 1)
                pool.wait_ge(b_ready, l + 1)
                distances(l, 1)
                distances(l, 2)
                for j in range(1, 9):
                    weigh_keys(l, j)
                    if j + 2 <= 8:
                        distances(l, j + 2)
                    if j == 6:
                        pool.wait_ge(dec_ready, l * 2 + 2)
                        G.tensor_tensor(dec_sq, dec[:], dec[:], ALU.mult).then_inc(dec2_ready, 1)
                pool.wait_ge(mult_ready, l + 1)
                pool.wait_ge(lin_part, l + 1)
                G.tensor_tensor(lin[:], lin[:], rt[:], ALU.mult).then_inc(lin_ready, 1)
                pool.wait_ge(v_mean, l + 1)
                mean = v_stat[:, 0:8].unsqueeze(2).to_broadcast([P, 8, 64])
                vg = v_z[:].rearrange("p t (g c) -> p (t g) c", c=64)
                G.tensor_tensor(vg, vg, mean, ALU.subtract).then_inc(v_cent, 1)
                pool.wait_ge(v_var, l + 1)
                G.tensor_tensor(v_stat[:, 16:24], v_stat[:, 8:16], neg_half[:, 0:8], ALU.pow).then_inc(v_rstd, 1)
                pool.wait_ge(v_rstd, l + 1)
                pool.wait_ge(v_sq, l + 1)
                rstd = v_stat[:, 16:24].unsqueeze(2).to_broadcast([P, 8, 64])
                G.tensor_tensor(vg, vg, rstd, ALU.mult).then_inc(v_ready, 1)
                pool.wait_ge(h_ready, l * 2 + 2)
                pool.wait_ge(gate_gelu, l + 1)
                G.tensor_tensor(y_bc[:, 0:2, :], xc[:], gate_z, ALU.mult).then_inc(yb_ready, 1)
                pool.wait_ge(yb_ready, l + 1)
                pool.wait_ge(yc_ready, l + 1)
                pool.wait_ge(v_var, l + 1)
                G.tensor_tensor(ysq[:], y_bc[:], y_bc[:], ALU.mult).then_inc(ysq_ready, 1)
                pool.wait_ge(varbc, l + 1)
                G.tensor_tensor(stat_bc[:], stat_bc[:], neg_half[:], ALU.pow).then_inc(rstdbc, 1)
                pool.wait_ge(vara, l + 1)
                G.tensor_tensor(stat_a[:], stat_a[:], neg_half[:, 0:8], ALU.pow).then_inc(rstda, 1)

            G.memset(neg_half[:], -0.5).then_inc(setup_pool, 1)
            G.memset(reset[:], 1.0).then_inc(setup_pool, 1)
            pool.wait_ge(setup_pool, 2)
            G.memset(reset[:].rearrange("p (n s) -> p n s", s=SUB)[:, :, 0:1], 0.0)
            G.memset(scores[:], 0.0).then_inc(setup_pool, 1)
            with pool.Fori(0, DEPTH) as l:
                pool.wait_ge(x_ready, l * 12 + 1)
                for b in range(4):
                    G.tensor_tensor(xsq[:, 2 * b:2 * b + 2, :], x[:, 2 * b:2 * b + 2, :], x[:, 2 * b:2 * b + 2, :],
                                    ALU.mult).then_inc(xsq_ready, 1)
                rsqrt_tok(l * 3)
                squares(l * 3 + 1, l * 12)
                mixer(l)
                squares(l * 3 + 2, l * 12 + 4)
            squares(3 * DEPTH, DEPTH * 12 - 4)

        @block.vector
        def _(dve):
            V = nc.vector

            def lo(slot, use):
                dve.wait_ge(hi_ready[slot], use + 1)
                V.tensor_tensor(wlo[slot][:], raw[slot][:], whi[slot][:].bitcast(F32), ALU.subtract)\
                    .then_inc(lo_ready[slot], 1)

            def split_x(norm, col, m):
                dve.wait_ge(xhi_ready, norm * KT + m + 1)
                V.scalar_tensor_tensor(xlo[:, m, :], x[:, m, :], par[:, col + m:col + m + 1],
                                       xhi[:, m, :].bitcast(F32), ALU.mult, ALU.subtract).then_inc(xlo_ready, 1)

            def residual(update, b, factor):
                dve.wait_ge(acc_done, update * 4 + b + 1)
                V.scalar_tensor_tensor(x[:, 2 * b:2 * b + 2, :], acc[:, 2 * b:2 * b + 2, :], factor,
                                       x[:, 2 * b:2 * b + 2, :], ALU.mult, ALU.add).then_inc(x_ready, 1)

            def residual_and_split(update, norm, col, factor):
                residual(update, 0, factor)
                for b in range(1, 4):
                    residual(update, b, factor)
                    split_x(norm, col, 2 * b - 2)
                    split_x(norm, col, 2 * b - 1)
                split_x(norm, col, 6)
                split_x(norm, col, 7)

            def norm_stats(norm):
                dve.wait_ge(normsum_ready, norm + 1)
                V.tensor_scalar(tokvar[:], normsum, 1.0 / D, EPS, ALU.mult, ALU.add).then_inc(var_ready, 1)
                dve.wait_ge(rtok_ready, norm + 1)
                V.tensor_copy(rinv_rows[:], rinv_tok[:].unsqueeze(2).to_broadcast([P, TT, P])).then_inc(rrows_ready, 1)
                dve.wait_ge(rps_ready, norm + 1)
                V.tensor_copy(rinv[:], rinv_ps).then_inc(rinv_ready, 1)

            rinv2 = rinv[:].unsqueeze(1).to_broadcast([P, 2, SEQ])

            def swiglu(l, f, norm):
                g, u, d = ROLES[f]
                done = l * (2 * FCH) + f * FCH

                def gate(i):
                    dve.wait_ge(rinv_ready, norm + 1)
                    dve.wait_ge(chunk_used[g], use_f(l, f, g, i) + 2)
                    V.tensor_tensor(gsc[:], zb[0], rinv2, ALU.mult).then_inc(gsc_ready, 1)

                def gated(i):
                    dve.wait_ge(chunk_used[u], use_f(l, f, u, i) + 2)
                    dve.wait_ge(gact_ready, done + i + 1)
                    V.tensor_tensor(up[:], zb[1], gact[:], ALU.mult).then_inc(up_ready, 1)
                    dve.wait_ge(up_ready, done + i + 1)
                    V.tensor_tensor(act_f[:], up[:], rinv2, ALU.mult).then_inc(actf_ready, 1)

                def split_act(i):
                    dve.wait_ge(ahi_ready, done + i + 1)
                    V.tensor_tensor(alo[:], act_f[:], ahi[:].bitcast(F32), ALU.subtract).then_inc(alo_ready, 1)

                norm_stats(norm)
                with dve.Fori(0, FCH - 1) as i:
                    gate(i)
                    lo(g, use_f(l, f, g, i + 1))
                    gated(i)
                    lo(u, use_f(l, f, u, i + 1))
                    split_act(i)
                    lo(d, use_f(l, f, d, i))
                gate(FCH - 1)
                gated(FCH - 1)
                split_act(FCH - 1)
                lo(d, use_f(l, f, d, FCH - 1))

            def mixer(l, norm):
                def evac(n, dst, signal):
                    dve.wait_ge(rinv_ready, norm + 1)
                    dve.wait_ge(chunk_used[n % 3], use_in(l, n) + 2)
                    V.tensor_tensor(dst, zb[n % 2], rinv2, ALU.mult).then_inc(signal, 1)

                def freed(n, signal, value):
                    dve.wait_ge(signal, value)
                    dve.sem_inc(z_free[n % 2], 1)

                def lo_after(n):
                    m = n + 3
                    lo(m % 3, use_in(l, m) if m < N_IN else use_out(l, m - N_IN))

                def weigh_queries(j):
                    h = ((128,) + HALVES)[j - 1]
                    dve.wait_ge(exp_ready, l * 8 + j)
                    dve.wait_ge(q_ready, l * 2 + 2)
                    if j > 2:
                        dve.wait_ge(score_done, l * 9 + (j - 1))
                    sel = "p h (n two s) -> p (h n) two s"
                    o, e, q = (t[:].rearrange(sel, two=2, s=h)[:, :, 1, :] for t in (wqk[j % 2], dist[j % 2], qq))
                    V.tensor_tensor(o, e, q, ALU.mult).then_inc(wq_ready, 1)

                def keep(j):
                    kept = 0 if j == 0 else j - 1
                    which = len(HALVES) if j == 0 else j - 2
                    dve.wait_ge(score_done, l * 9 + j + 1)
                    dve.sem_inc(keep_begun, 1)
                    m = mask[:, which, :].unsqueeze(1).to_broadcast([P, HEADS * TT, P])
                    V.copy_predicated(scores[:], m, sc_ps).then_inc(score_kept, 1)
                    dve.wait_ge(score_kept, l * 8 + kept + 1)

                def conv():
                    for m in range(2):
                        V.tensor_scalar(xc[:, m, :], xpad[:, m, 0:SEQ], par[:, C_CW + m:C_CW + m + 1],
                                        par[:, C_CB + m:C_CB + m + 1], ALU.mult, ALU.add).then_inc(conv_step, 1)
                    for tap in range(1, 4):
                        dve.wait_ge(conv_step, l * 6 + 2 * tap)
                        for m in range(2):
                            c = C_CW + 2 * tap + m
                            V.scalar_tensor_tensor(xc[:, m, :], xpad[:, m, tap:tap + SEQ], par[:, c:c + 1],
                                                   xc[:, m, :], ALU.mult, ALU.add)\
                                .then_inc(conv_step if tap < 3 else xc_ready, 1)

                def step(n):
                    if n in (0, 1):
                        evac(n, fz[:, 2 * n:2 * n + 2, :], f_evac)
                        freed(n, f_evac, l * 2 + n + 1)
                    if n in (2, 3):
                        evac(n, qz[:, 2 * n - 4:2 * n - 2, :], q_evac)
                        freed(n, q_evac, l * 2 + (n - 1))
                    if n == 4:
                        evac(n, xpad[:, :, 3:3 + SEQ], xb_evac)
                        freed(n, xb_evac, l + 1)
                    if n == 5:
                        evac(n, gate_z, gate_evac)
                        freed(n, gate_evac, l + 1)
                    if n == 9:
                        evac(n, u_z, u_evac)
                        freed(n, u_evac, l + 1)
                    if n in (10, 11):
                        evac(n, gz[:, 2 * n - 20:2 * n - 18, :], g_evac)
                        freed(n, g_evac, l * 2 + (n - 9))
                    lo_after(n)
                    if n == 1:
                        dve.wait_ge(f_sig, l * 2 + 2)
                        for h in range(HEADS):
                            V.tensor_scalar(fz[:, h, :], fz[:, h, :], par[:, C_OML + h:C_OML + h + 1],
                                            par[:, C_LB + h:C_LB + h + 1], ALU.mult, ALU.add).then_inc(forget_ready, 1)
                        dve.wait_ge(forget_ready, l * 4 + 4)
                        V.tensor_scalar(kk[:], fz[:], -1.0, 1.0, ALU.mult, ALU.add).then_inc(k_ready, 1)
                        dve.wait_ge(k_ready, l + 1)
                        V.tensor_scalar(fz[:], fz[:], 2.0 ** -63, None, ALU.max).then_inc(clamp_ready, 1)
                    if n == 3:
                        dve.wait_ge(logf_ready, l + 1)
                        V.tensor_tensor_scan(bc[:].rearrange("p h t -> p (h t)"), reset[:],
                                             fz[:].rearrange("p h t -> p (h t)"), 0.0, ALU.mult, ALU.add)\
                            .then_inc(b_ready, 1)
                    if n == 4:
                        conv()
                        weigh_queries(1)
                        keep(0)
                    if 5 <= n <= 11:
                        weigh_queries(n - 3)
                        if n > 5:
                            keep(n - 4)
                    if n == 7:
                        dve.wait_ge(rg_tanh, l * 4 + 4)
                        V.scalar_tensor_tensor(lin[:], gt[:], 1.0, xc[:], ALU.add, ALU.mult).then_inc(lin_part, 1)
                    if n == 9:
                        dve.wait_ge(dec2_ready, l + 1)
                        dve.wait_ge(th_ready, l * 2 + 2)
                        V.scalar_tensor_tensor(th[:], dec_sq, 1.0, th[:], ALU.add, ALU.mult)\
                            .then_inc(mult2_ready, 1)

                lo(2, use_in(l, 2))
                dve.wait_ge(small_landed, l * 48 + 48)
                V.tensor_tensor(wt[:], wt[:], tri[:].unsqueeze(1).to_broadcast([P, 4, P]), ALU.mult)\
                    .then_inc(wt_masked, 1)
                norm_stats(norm)
                for n in range(N_IN):
                    step(n)
                vg = v_z[:].rearrange("p t (g c) -> p (t g) c", c=64)
                dve.wait_ge(v_gelu, l + 1)
                V.reduce_sum(v_stat[:, 0:8], vg, AX.X).then_inc(v_part, 1)
                dve.wait_ge(v_part, l * 2 + 1)
                V.tensor_scalar(v_stat[:, 0:8], v_stat[:, 0:8], 1.0 / 64, None, ALU.mult).then_inc(v_mean, 1)
                dve.wait_ge(v_sq, l + 1)
                V.reduce_sum(v_stat[:, 8:16], ysq[:, 0:2, :].rearrange("p j (g c) -> p (j g) c", c=64), AX.X)\
                    .then_inc(v_part, 1)
                dve.wait_ge(v_part, l * 2 + 2)
                V.tensor_scalar(v_stat[:, 8:16], v_stat[:, 8:16], 1.0 / 64, EPS, ALU.mult, ALU.add)\
                    .then_inc(v_var, 1)
                keep(8)
                dve.wait_ge(lin_ready, l + 1)
                for m in range(2):
                    V.tensor_tensor_scan(xc[:, m, :], dec[:, m, :], lin[:, m, :], 0.0, ALU.mult, ALU.add)\
                        .then_inc(h_ready, 1)
                dve.wait_ge(g_tanh, l + 1)
                V.scalar_tensor_tensor(gz[:], qs[:], 1.0, gz[:], ALU.add, ALU.mult).then_inc(gs_ready, 1)
                dve.wait_ge(u_gelu, l + 1)
                dve.wait_ge(z_done, l + 1)
                V.tensor_tensor(y_bc[:, 2:4, :], z_ps, u_z, ALU.mult).then_inc(yc_ready, 1)
                dve.wait_ge(sumbc_done, l + 1)
                V.tensor_scalar(stat_bc[:], sum_bc, 1.0 / 64, EPS, ALU.mult, ALU.add).then_inc(varbc, 1)
                dve.wait_ge(rstdbc, l + 1)
                V.tensor_copy(rows, stat_bc[:].unsqueeze(2).to_broadcast([P, 16, 64])).then_inc(rowsbc, 1)
                dve.wait_ge(osq_ready, l + 1)
                dve.wait_ge(gs_ready, l + 1)
                for h in range(HEADS):
                    ins = V.scalar_tensor_tensor(gz[:, h, :], o_ps[:, h, :], par[:, C_HHN + h:C_HHN + h + 1],
                                                 gz[:, h, :], ALU.mult, ALU.mult)
                ins.then_inc(og_ready, 1)
                dve.wait_ge(rbc_done, l + 1)
                for j in range(4):
                    V.scalar_tensor_tensor(ysq[:, j, :], y_bc[:, j, :], par[:, C_GBC + j:C_GBC + j + 1],
                                           rbc_ps[:, j, :], ALU.mult, ALU.mult).then_inc(nbc_ready, 1)
                dve.wait_ge(suma_done, l + 1)
                V.tensor_scalar(stat_a[:], sum_a, 1.0 / 128, EPS, ALU.mult, ALU.add).then_inc(vara, 1)
                dve.wait_ge(yhbc, l + 1)
                V.tensor_tensor(ylo[:, 4:8, :], ysq[:], yhi[:, 4:8, :].bitcast(F32), ALU.subtract).then_inc(ylbc, 1)
                dve.wait_ge(rstda, l + 1)
                V.tensor_copy(rows_a,
                              stat_a[:].unsqueeze(2).to_broadcast([P, 8, P])).then_inc(rowsa, 1)
                dve.wait_ge(ra_done, l + 1)
                dve.wait_ge(og_ready, l + 1)
                V.tensor_tensor(osq[:], ra_ps, gz[:], ALU.mult).then_inc(na_ready, 1)
                dve.wait_ge(yha, l + 1)
                V.tensor_tensor(ylo[:, 0:4, :], osq[:], yhi[:, 0:4, :].bitcast(F32), ALU.subtract).then_inc(yla, 1)
                lo(0, use_out(l, 3))
                lo(1, use_f(l, 1, 1, 0))
                lo(2, use_f(l, 1, 2, 0))

            for slot in range(3):
                dve.sem_inc(lo_ready[slot], 1)
            V.memset(ones_col[:], 1.0)
            V.memset(ones_row[:], 1.0)
            V.memset(half_ones[:], 0.0).then_inc(setup_chain, 1)
            dve.wait_ge(setup_chain, 1)
            V.memset(half_ones[0:64, 0:1], 1.0)
            V.memset(half_ones[64:128, 1:2], 1.0)
            dve.wait_ge(const_landed, 16 * N_CONST)
            V.tensor_copy(mask[:].rearrange("p a t -> p (a t)"), bc[:].rearrange("p h t -> p (h t)"))
            V.memset(xpad[:, :, 0:3], 0.0).then_inc(setup_vec, 1)
            lb0, lb1 = par_all[:, 0, C_LBL:C_LBL + 4], par_all[:, 1, C_LBL:C_LBL + 4]
            t0 = stat_bc[:, 0:4]
            t1 = stat_bc[:, 4:8]

            def after(ins):
                chain[0] += 1
                ins.then_inc(setup_chain, 1)
                dve.wait_ge(setup_chain, chain[0])

            chain = [1]
            after(V.tensor_tensor(t0, lb0, lb1, ALU.max))
            V.tensor_tensor(lb0, lb0, t0, ALU.subtract)
            V.tensor_tensor(lb1, lb1, t0, ALU.subtract).then_inc(setup_vec, 1)
            dve.wait_ge(setup_act, 5)
            after(V.tensor_tensor(t0, lb0, lb1, ALU.add))
            after(V.reciprocal(t0, t0))
            V.tensor_tensor(lb0, lb0, t0, ALU.mult)
            after(V.tensor_tensor(lb1, lb1, t0, ALU.mult))
            V.tensor_tensor(par_all[:, 0, C_LB:C_LB + 4], lb0, lb0, ALU.subtract)
            after(V.tensor_tensor(t1, lb0, lb1, ALU.add))
            after(V.tensor_tensor(par_all[:, 1, C_LB:C_LB + 4], t1, lb0, ALU.subtract))
            V.tensor_scalar(par_all[:, :, C_OML:C_OML + 4], par_all[:, :, C_LB:C_LB + 4], -1.0, 1.0, ALU.mult, ALU.add)
            s0 = v_stat[:, 0:4].rearrange("p (l c) -> p l c", l=DEPTH)
            s1 = v_stat[:, 4:8].rearrange("p (l c) -> p l c", l=DEPTH)
            c4 = par_all[:, :, C_C4:C_C4 + 2]
            after(V.tensor_tensor(c4, s0, s1, ALU.add))
            V.tensor_scalar(c4, c4, -4.0, None, ALU.mult)
            V.tensor_scalar(par_all[:, :, C_HBA:C_HBA + 4], par_all[:, :, C_BA:C_BA + 4], 0.5, None, ALU.mult)
            after(V.tensor_scalar(par_all[:, :, C_HHN:C_HHN + 4], par_all[:, :, C_HN:C_HN + 4], 0.5, None, ALU.mult))
            dve.wait_ge(setup_pool, 3)
            dve.wait_ge(x_landed, 16)
            dve.sem_inc(x_ready, 1)

            with dve.Fori(0, DEPTH) as l:
                V.tensor_copy(par[:], par_all[:, ds(l, 1), :].rearrange("p a c -> p (a c)")).then_inc(par_ready, 1)
                dve.wait_ge(par_ready, l + 1)
                lo(1, use_f(l, 0, 1, 0))
                for m in range(KT):
                    split_x(l * 3, C_N1, m)
                lo(0, use_f(l, 0, 0, 0))
                swiglu(l, 0, l * 3)
                lo(0, use_in(l, 0))
                lo(1, use_in(l, 1))
                residual_and_split(l * 3, l * 3 + 1, C_NM, 0.5)
                mixer(l, l * 3 + 1)
                residual_and_split(l * 3 + 1, l * 3 + 2, C_N2, 1.0)
                swiglu(l, 1, l * 3 + 2)
                for b in range(4):
                    residual(l * 3 + 2, b, 0.5)
            norm_stats(3 * DEPTH)
            dve.wait_ge(rinv_ready, 3 * DEPTH + 1)
            for m in range(KT):
                ins = V.scalar_tensor_tensor(xsq[:, m, :], x[:, m, :], gain_fin[:, m:m + 1], rinv[:],
                                             ALU.mult, ALU.mult)
                if m % 4 == 3:
                    ins.then_inc(outt_ready, 1)


def chunks_of_columns(w, order=None):
    n = w.shape[1] // CW
    c = w.reshape(KT, P, n, CW).transpose(2, 1, 0, 3).reshape(n, P, CHUNK)
    return c if order is None else c[list(order)]


def chunks_of_rows(w, order=None):
    n = w.shape[0] // (2 * P)
    c = w.reshape(n, 2, P, D).transpose(0, 2, 1, 3).reshape(n, P, CHUNK)
    return c if order is None else c[list(order)]


def swiglu_chunks(wg, wu, wd):
    g, u, d = chunks_of_columns(wg), chunks_of_columns(wu), chunks_of_rows(wd)
    out = [g[0], u[0]]
    for i in range(1, FCH):
        out += [g[i], u[i], d[i - 1]]
    return out + [d[FCH - 1]]


def kernel(**inputs):
    import concourse.bacc as bacc
    from concourse import mybir
    from concourse.bass_utils import run_bass_kernel_spmd

    a = {k: np.asarray(v) for k, v in inputs.items()}
    f32 = np.float32
    stream = np.empty((DEPTH * PER_LAYER, P, CHUNK), f32)
    at = 0
    for l in range(DEPTH):
        parts = swiglu_chunks(a["ffn1_wg"][l], a["ffn1_wu"][l], a["ffn1_wd"][l])
        parts += list(chunks_of_columns(a["w_in"][l], IN_ORDER)) + list(chunks_of_rows(a["w_out"][l], OUT_ORDER))
        parts += swiglu_chunks(a["ffn2_wg"][l], a["ffn2_wu"][l], a["ffn2_wd"][l])
        for part in parts:
            stream[at] = part
            at += 1

    def tiles(v):
        return v.reshape(-1, P).T

    params = np.zeros((P, DEPTH, N_PAR), f32)
    bd = np.zeros((P, DEPTH, 4, P), f32)
    for l in range(DEPTH):
        for c, v in ((C_N1, a["ffn1_norm"]), (C_NM, a["mix_norm"]), (C_N2, a["ffn2_norm"]), (C_HN, a["hgrn_norm"]),
                     (C_CW, a["conv_w"]), (C_CB, a["conv_b"]), (C_BA, a["lru_ba"]), (C_BX, a["lru_bx"]),
                     (C_LAM, a["lru_lambda"]), (C_GBC, a["lru_norm"]), (C_GBC + 2, a["sgu_norm"]),
                     (C_LBL, a["hgrn_lb_logits"])):
            t = tiles(v[l])
            params[:, l, c:c + t.shape[1]] = t
        for which, w in enumerate((a["lru_wa"], a["lru_wx"])):
            for blk in range(4):
                o = 64 * (blk % 2)
                bd[o:o + 64, l, 2 * which + blk // 2, o:o + 64] = w[l, blk]
    s = np.arange(P)[:, None]
    t = np.arange(P)[None, :]
    masks = np.zeros((P, len(HALVES) + 1, P), f32)
    for n, h in enumerate(HALVES):
        masks[:, n] = (s // (2 * h) == t // (2 * h)) & (s % (2 * h) < h) & (t % (2 * h) >= h)
    masks[:, -1] = s == t
    arrays = {
        "x_t": np.ascontiguousarray(a["x"][0].T.reshape(KT, P, SEQ).transpose(1, 0, 2)),
        "wstream": stream,
        "params": params,
        "gain_out": np.ascontiguousarray(tiles(a["final_norm"])),
        "block_diag": bd.reshape(P, DEPTH, 4 * P),
        "sgu_wt": np.ascontiguousarray(a["sgu_w"].transpose(3, 0, 1, 2)).reshape(P, DEPTH, 4 * P),
        "sgu_bias": np.ascontiguousarray(a["sgu_b"]).reshape(1, DEPTH, 4 * P),
        "identity": np.eye(P, dtype=f32),
        "masks": masks.reshape(P, -1),
        "causal": (s <= t).astype(f32),
    }
    nc = bacc.Bacc("TRN2", target_bir_lowering=False, num_devices=1)
    args = [nc.dram_tensor(k, v.shape, mybir.dt.from_np(v.dtype), kind="ExternalInput").ap()
            for k, v in arrays.items()]
    out = nc.dram_tensor("out_t", (P, KT, SEQ), mybir.dt.float32, kind="ExternalOutput").ap()
    build(nc, *args, out)
    got = run_bass_kernel_spmd(nc, [arrays], core_ids=[0]).results[0]["out_t"]
    return np.ascontiguousarray(got.transpose(1, 0, 2).reshape(D, SEQ).T)[None]
```

```python
import numpy as np

DEPTH, D, SEQ, DFF = 2, 1024, 256, 2816
P = 128
KT = D // P
TT = SEQ // P
CW = 256
CHUNK = KT * CW
FCH = DFF // CW
HEADS = 4
DA, DB, DC = 512, 256, 256
SUB = 64
EPS = 1e-6
N_IN, N_OUT = 12, 4
PER_LAYER = 2 * 3 * FCH + N_IN + N_OUT
IN_ORDER = (2, 3, 0, 1, 8, 9, 4, 5, 11, 10, 6, 7)
OUT_ORDER = (2, 3, 0, 1)
HALVES = (64, 32, 16, 8, 4, 2, 1)

C_N1, C_NM, C_N2, C_HN, C_CW, C_CB, C_BA, C_BX, C_LAM, C_GBC, C_LBL = 0, 8, 16, 24, 28, 36, 38, 40, 42, 44, 48
N_PAR = 52
C_LB, C_OML, C_C4, C_HBA, C_HBX = 52, 56, 60, 62, 64
N_ALL = 66
N_CONST = 3
VEC_STEPS = 10


def build(nc, x_in, wstream, params, gain_out, block_diag, sgu_wt, sgu_bias, identity, masks, causal, out):
    import concourse.bass as bass
    from concourse import mybir
    from contextlib import ExitStack

    F32, F32R, U8 = mybir.dt.float32, mybir.dt.float32r, mybir.dt.uint8
    ALU, ACT, AX = mybir.AluOpType, mybir.ActivationFunctionType, mybir.AxisListType
    ds = bass.ds

    with ExitStack() as ctx:
        def sb(name, shape, dt=F32):
            return ctx.enter_context(nc.sbuf_tensor(name, shape, dt))

        def sem(name):
            return ctx.enter_context(nc.semaphore(name))

        raw = [sb(f"raw{s}", [P, CHUNK]) for s in range(3)]
        whi = [sb(f"whi{s}", [P, CHUNK], F32R) for s in range(3)]
        wlo = [sb(f"wlo{s}", [P, CHUNK], F32R) for s in range(3)]
        x = sb("x", [P, KT, SEQ])
        xhi = sb("xhi", [P, KT, SEQ], F32R)
        xlo = sb("xlo", [P, KT, SEQ], F32R)
        yhi = sb("yhi", [P, KT, SEQ], F32R)
        ylo = sb("ylo", [P, KT, SEQ], F32R)
        xsq = sb("xsq", [P, KT, SEQ])
        rinv = sb("rinv", [P, SEQ])
        rinv_tok = sb("rinv_tok", [P, TT])
        tokvar = sb("tokvar", [P, TT])
        rinv_rows = sb("rinv_rows", [P, TT, P])
        par_all = sb("par_all", [P, DEPTH, N_PAR])
        par = sb("par", [P, N_ALL])
        vec = sb("vec", [P, 24])
        gain_fin = sb("gain_fin", [P, KT])
        bd = sb("bd", [P, 4, P])
        wt = sb("wt", [P, 4, P])
        tri = sb("tri", [P, P])
        sbias = sb("sbias", [1, 4, P])
        ident = sb("ident", [P, P])
        mask = sb("mask", [P, len(HALVES) + 1, P], U8)
        ones_col = sb("ones_col", [P, 1])
        half_ones = sb("half_ones", [P, 2])
        eps_col = sb("eps_col", [P, 1])
        ones_row = sb("ones_row", [1, 64])
        reset = sb("reset", [P, HEADS * SEQ])
        neg_half = sb("neg_half", [P, 8])
        ahi = sb("ahi", [P, 2, SEQ], F32R)
        alo = sb("alo", [P, 2, SEQ], F32R)
        ahi_last, alo_last = yhi[:, 0:2, :], ylo[:, 0:2, :]
        fz = sb("fz", [P, HEADS, SEQ])
        kk = sb("kk", [P, HEADS, SEQ])
        qz = sb("qz", [P, HEADS, SEQ])
        qs = sb("qs", [P, HEADS, SEQ])
        qq = sb("qq", [P, HEADS, SEQ])
        bc = sb("bc", [P, HEADS, SEQ])
        dist = [sb(f"dist{i}", [P, HEADS, SEQ]) for i in range(2)]
        wqk = [sb(f"wqk{i}", [P, HEADS, SEQ]) for i in range(2)]
        scores = sb("scores", [P, HEADS * TT, P])
        cross = sb("cross", [P, HEADS, P])
        vals = sb("vals", [P, TT, DA])
        gz = fz
        osq = kk
        gate_z, u_z = qz[:, 0:2, :], qz[:, 2:4, :]
        inv_a = sb("inv_a", [P, TT, HEADS])
        inv_bc = sb("inv_bc", [P, 2, TT, 2, 2])
        rows_bc = dist[1][:].rearrange("p (c t) (j s) -> p c t j s", c=2, s=P)
        rows_a = dist[0][:].rearrange("p (t a) (b s) -> p t (a b) s", t=TT, s=P)
        xpad = sb("xpad", [P, 2, 3 + SEQ])
        xc = sb("xc", [P, 2, SEQ])
        rt = sb("rt", [P, 2, SEQ])
        gt = sb("gt", [P, 2, SEQ])
        th = sb("th", [P, 2, SEQ])
        dec = sb("dec", [P, 2, SEQ])
        lin = sb("lin", [P, 2, SEQ])
        v_z = sb("v_z", [P, TT, DC])
        v_stat = sb("v_stat", [P, 24])
        y_bc = bc
        ysq = qq
        dec_sq = xsq[:, 0:2, :]
        v_squares = th
        gsc, gact, up, act_f = rt, gt, th, dec

        ps = ctx.enter_context(nc.psum_tensor("ps", [P, 8 * 512], F32))

        def bank(b, n=1):
            return ps[:, 512 * b:512 * (b + n)]

        acc = bank(0, 4).rearrange("p (m t) -> p m t", t=SEQ)
        zb = [bank(4).rearrange("p (m t) -> p m t", t=SEQ), bank(5).rearrange("p (m t) -> p m t", t=SEQ)]
        normsum = ps[:, 6 * 512:6 * 512 + TT]
        rinv_ps = ps[:, 6 * 512 + 256:7 * 512]
        sc_ps = [bank(b, 2).rearrange("p (a t) -> p a t", t=P) for b in (0, 2)]
        cross_ps = bank(7).rearrange("p (a t) -> p a t", t=P)
        gate_ps = bank(2, 2).rearrange("p (a m t) -> p a m t", a=2, t=SEQ)
        o_ps = bank(4, 2).rearrange("p (h t) -> p h t", t=SEQ)
        z_ps = bank(7).rearrange("p (j t) -> p j t", t=SEQ)
        sumsq_bc = ps[:, 6 * 512 + 8:6 * 512 + 24].rearrange("p (c t j s) -> p c t j s", c=2, t=TT, j=2)
        sumsq_a = ps[:, 6 * 512 + 24:6 * 512 + 32].rearrange("p (t h) -> p t h", t=TT)
        spread_bc_ps = bank(7).rearrange("p (j t) -> p j t", t=SEQ)
        spread_a_ps = o_ps

        const_landed, x_landed, out_landed = sem("const_landed"), sem("x_landed"), sem("out_landed")
        v_part = sem("v_part")
        ident_landed, par_landed = sem("ident_landed"), sem("par_landed")
        small_landed, wt_masked = sem("small_landed"), sem("wt_masked")
        landed = [sem(f"landed{s}") for s in range(3)]
        hi_ready = [sem(f"hi_ready{s}") for s in range(3)]
        lo_ready = [sem(f"lo_ready{s}") for s in range(3)]
        chunk_used = [sem(f"chunk_used{s}") for s in range(3)]
        ones_made, setup_pool = sem("ones_made"), sem("setup_pool")
        par_ready = sem("par_ready")
        vec_act, vec_dve = sem("vec_act"), sem("vec_dve")
        x_ready = sem("x_ready")
        xhi_ready, xlo_ready = sem("xhi_ready"), sem("xlo_ready")
        xsq_ready = sem("xsq_ready")
        normsum_ready, var_ready, rtok_ready = sem("normsum_ready"), sem("var_ready"), sem("rtok_ready")
        rrows_ready, rps_ready, rinv_ready = sem("rrows_ready"), sem("rps_ready"), sem("rinv_ready")
        gsc_ready, gact_ready, up_ready = sem("gsc_ready"), sem("gact_ready"), sem("up_ready")
        actf_ready, ahi_ready, alo_ready = sem("actf_ready"), sem("ahi_ready"), sem("alo_ready")
        acc_done = sem("acc_done")
        z_free = [sem("z_free0"), sem("z_free1")]
        f_evac, f_sig, forget_ready, k_ready, clamp_ready = (
            sem("f_evac"), sem("f_sig"), sem("forget_ready"), sem("k_ready"), sem("clamp_ready"))
        logf_ready, b_ready = sem("logf_ready"), sem("b_ready")
        q_evac, q_sig, q_ready = sem("q_evac"), sem("q_sig"), sem("q_ready")
        dist_part = sem("dist_part")
        dist_ready, exp_ready = sem("dist_ready"), sem("exp_ready")
        wq_ready, wk_ready = sem("wq_ready"), sem("wk_ready")
        score_done, score_kept = sem("score_done"), sem("score_kept")
        cross_kept, keep_begun = sem("cross_kept"), sem("keep_begun")
        vals_ready = sem("vals_ready")
        xb_evac, conv_step, xc_ready = sem("xb_evac"), sem("conv_step"), sem("xc_ready")
        gates_done, rg_tanh, th_ready = sem("gates_done"), sem("rg_tanh"), sem("th_ready")
        dec_ready, dec2_ready, mult2_ready, mult_ready = (
            sem("dec_ready"), sem("dec2_ready"), sem("mult2_ready"), sem("mult_ready"))
        lin_part, lin_ready, h_ready, yb_ready = sem("lin_part"), sem("lin_ready"), sem("h_ready"), sem("yb_ready")
        gate_evac, gate_gelu, u_evac, u_gelu = sem("gate_evac"), sem("gate_gelu"), sem("u_evac"), sem("u_gelu")
        v_evac, v_gelu, v_mean, v_cent, v_sq, v_var, v_rstd, v_ready = (
            sem("v_evac"), sem("v_gelu"), sem("v_mean"), sem("v_cent"), sem("v_sq"), sem("v_var"),
            sem("v_rstd"), sem("v_ready"))
        z_done, yc_ready = sem("z_done"), sem("yc_ready")
        ysq_ready, sumbc_done = sem("ysq_ready"), sem("sumbc_done")
        rms_bc, inv_bc_ready, nbc_ready = sem("rms_bc"), sem("inv_bc_ready"), sem("nbc_ready")
        rows_bc_ready, spread_bc_done = sem("rows_bc_ready"), sem("spread_bc_done")
        rows_a_ready, spread_a_done = sem("rows_a_ready"), sem("spread_a_done")
        yhbc, ylbc = sem("yhbc"), sem("ylbc")
        g_evac, g_sig, gs_ready = sem("g_evac"), sem("g_sig"), sem("gs_ready")
        o_done, osq_ready, og_ready = sem("o_done"), sem("osq_ready"), sem("og_ready")
        suma_done, rms_a, inv_a_ready = sem("suma_done"), sem("rms_a"), sem("inv_a_ready")
        na_ready, yha, yla = sem("na_ready"), sem("yha"), sem("yla")
        outt_ready = sem("outt_ready")

        ROLES = ((0, 1, 2), (2, 0, 1))
        USED_F = (FCH + 1, FCH, FCH - 1)
        N_MIX = N_IN + N_OUT
        USED_MIX = [len(range((s - 1) % 3, N_MIX, 3)) for s in range(3)]
        USES = [USED_F[s] + USED_MIX[s] + USED_F[ROLES[1].index(s)] for s in range(3)]

        def use_f(l, f, slot, i):
            return l * USES[slot] + (i + f * (USED_F[slot] + USED_MIX[slot]))

        def slot_mix(j):
            return (j + 1) % 3

        def use_mix(l, j):
            return l * USES[slot_mix(j)] + (USED_F[slot_mix(j)] + j // 3)


        block = ctx.enter_context(nc.Block())

        @block.sync
        def _(sp):
            def load(slot, use, chunk):
                sp.wait_ge(lo_ready[slot], use + 1)
                sp.dma_start(raw[slot][:], wstream[ds(chunk, 1)].rearrange("a p c -> p (a c)"))\
                    .then_inc(landed[slot], 16)

            def load_swiglu(l, f, first):
                g, u, d = ROLES[f]
                load(u, use_f(l, f, u, 0), first + 1)
                with sp.Fori(0, FCH - 1) as i:
                    load(g, use_f(l, f, g, i + 1), first + i * 3 + 2)
                    load(u, use_f(l, f, u, i + 1), first + i * 3 + 3)
                    load(d, use_f(l, f, d, i), first + i * 3 + 4)
                load(g, use_f(l, f, g, FCH), first + (3 * FCH - 1))

            load(0, 0, 0)
            sp.dma_start(x[:], x_in).then_inc(x_landed, 16)
            with sp.Fori(0, DEPTH) as l:
                load_swiglu(l, 0, l * PER_LAYER)
                for j in range(N_MIX):
                    load(slot_mix(j), use_mix(l, j), l * PER_LAYER + (3 * FCH + j))
                    if j == 0:
                        sp.wait_ge(x_ready, l * 12 + 4)
                        for dst, src in ((bd, block_diag), (wt, sgu_wt), (sbias, sgu_bias)):
                            sp.dma_start(dst[:].rearrange("p a c -> p (a c)"),
                                         src[:, ds(l, 1), :].rearrange("p a c -> p (a c)")).then_inc(small_landed, 16)
                load(ROLES[1][0], use_f(l, 1, ROLES[1][0], 0), l * PER_LAYER + (3 * FCH + N_MIX))
                load_swiglu(l, 1, l * PER_LAYER + (3 * FCH + N_MIX))
                load(0, use_f(l + 1, 0, 0, 0), l * PER_LAYER + PER_LAYER)
            for h in range(2):
                sp.wait_ge(outt_ready, h + 1)
                sp.dma_start(out[:, 4 * h:4 * h + 4, :], xsq[:, 4 * h:4 * h + 4, :]).then_inc(out_landed, 16)
            sp.wait_ge(out_landed, 32)

        @block.tensor
        def _(pe):
            mm = nc.tensor.matmul

            def mm3(dst, wh, wl, mh, ml, start, stop, shared=False):
                mm(dst, wh, mh, start=start, stop=False, skip_group_check=shared)
                mm(dst, wh, ml, start=False, stop=False, skip_group_check=shared)
                return mm(dst, wl, mh, start=False, stop=stop, skip_group_check=shared)

            def cols(slot, dst, m, wait_x=None):
                wh = whi[slot][:].rearrange("p (k c) -> p k c", k=KT)
                wl = wlo[slot][:].rearrange("p (k c) -> p k c", k=KT)
                for k in range(KT):
                    if wait_x is not None:
                        pe.wait_ge(xlo_ready, wait_x + (k + 1))
                    last = mm3(dst[:, m, :], wh[:, k, m * P:m * P + P], wl[:, k, m * P:m * P + P],
                               xhi[:, k, :], xlo[:, k, :], k == 0, k == KT - 1)
                return last

            def toks(slot, dst, t):
                wh = whi[slot][:].rearrange("p (k c) -> p k c", k=KT)
                wl = wlo[slot][:].rearrange("p (k c) -> p k c", k=KT)
                for k in range(KT):
                    last = mm3(dst[:, t, :], xhi[:, k, t * P:t * P + P], xlo[:, k, t * P:t * P + P],
                               wh[:, k, :], wl[:, k, :], k == 0, k == KT - 1)
                return last

            def sum_squares(norm):
                pe.wait_ge(xsq_ready, norm * 4 + 4)
                for t in range(TT):
                    for k in range(KT):
                        last = mm(normsum[:, t:t + 1], xsq[:, k, t * P:t * P + P], ones_col[:],
                                  start=(k == 0), stop=(k == KT - 1))
                last.then_inc(normsum_ready, 1)

            def spread_rinv(norm):
                pe.wait_ge(rrows_ready, norm + 1)
                for t in range(TT):
                    last = mm(rinv_ps[:, t * P:t * P + P], rinv_rows[:, t, :], ident[:], start=True, stop=True)
                last.then_inc(rps_ready, 1)

            def first_chunk(slot, use, norm, dst):
                pe.wait_ge(lo_ready[slot], use + 2)
                cols(slot, dst, 0, wait_x=norm * KT)
                sum_squares(norm)
                cols(slot, dst, 1).then_inc(chunk_used[slot], 1)
                spread_rinv(norm)

            def accumulate(slot, use, hi_in, lo_in, first, last, between=None):
                pe.wait_ge(lo_ready[slot], use + 2)
                wh = whi[slot][:].rearrange("p (k n) -> p k n", k=2)
                wl = wlo[slot][:].rearrange("p (k n) -> p k n", k=2)

                def one(k, m, stop):
                    return mm3(acc[:, m, :], wh[:, k, m * P:m * P + P], wl[:, k, m * P:m * P + P],
                               hi_in[:, k, :], lo_in[:, k, :], first and k == 0 and m % 2 == 0, stop, shared=True)

                if not last:
                    for k in range(2):
                        for m in range(KT):
                            ins = one(k, m, False)
                        if between is not None and k == 0:
                            between()
                    ins.then_inc(chunk_used[slot], 1)
                else:
                    for b in range(4):
                        for m in (2 * b, 2 * b + 1):
                            for k in range(2):
                                ins = one(k, m, k == 1)
                        ins.then_inc(acc_done, 1)
                    mm(normsum[:, 0:1], ident[:], ones_col[:], start=True, stop=True).then_inc(chunk_used[slot], 1)

            def swiglu(l, f, norm):
                g, u, d = ROLES[f]
                done = l * (2 * FCH) + f * FCH
                first_chunk(g, use_f(l, f, g, 0), norm, zb[0])

                def up_chunk(i):
                    pe.wait_ge(lo_ready[u], use_f(l, f, u, i) + 2)
                    cols(u, zb[1], 0)
                    cols(u, zb[1], 1).then_inc(chunk_used[u], 1)

                def triple(i, first):
                    pe.wait_ge(lo_ready[g], use_f(l, f, g, i) + 2)
                    pe.wait_ge(gsc_ready, done + i)
                    cols(g, zb[0], 0)
                    cols(g, zb[0], 1).then_inc(chunk_used[g], 1)
                    pe.wait_ge(up_ready, done + i)
                    up_chunk(i)
                    pe.wait_ge(alo_ready, done + i)
                    accumulate(d, use_f(l, f, d, i - 1), ahi, alo, first, False)

                up_chunk(0)
                triple(1, True)
                with pe.Fori(2, FCH) as i:
                    triple(i, False)
                pe.wait_ge(alo_ready, done + FCH)
                accumulate(g, use_f(l, f, g, FCH), ahi_last, alo_last, False, True)

            def score(l, j):
                if j == 0:
                    pe.wait_ge(k_ready, l + 1)
                    pe.wait_ge(q_ready, l + 1)
                    left, right = kk, qq
                else:
                    pe.wait_ge(wq_ready, l * 8 + j)
                    pe.wait_ge(wk_ready, l * 8 + j)
                    left = right = wqk[j % 2]
                if j == 1:
                    for h in range(HEADS):
                        last = mm(cross_ps[:, h, :], left[:, h, 0:P], right[:, h, P:2 * P], start=True, stop=True)
                else:
                    if j == 8:
                        pe.wait_ge(rg_tanh, l * 4 + 4)
                    elif j > 1:
                        pe.wait_ge(score_kept, l * 8 + (j - 1))
                    for h in range(HEADS):
                        for t in range(TT):
                            last = mm(sc_ps[j // 8][:, h * TT + t, :], left[:, h, t * P:t * P + P],
                                      right[:, h, t * P:t * P + P], start=True, stop=True)
                last.then_inc(score_done, 1)

            def lru_gates(l):
                pe.wait_ge(small_landed, l * 48 + 48)
                pe.wait_ge(xc_ready, l * 2 + 2)
                for a in range(2):
                    for m in range(2):
                        last = mm(gate_ps[:, a, m, :], bd[:, 2 * a + m, :], xc[:, m, :], start=True, stop=True)
                last.then_inc(gates_done, 1)

            def sgu_mix(l):
                pe.wait_ge(v_ready, l + 1)
                pe.wait_ge(wt_masked, l + 1)
                pe.wait_ge(nbc_ready, l * 4 + 2)
                for grp in range(4):
                    lo_p = 64 * (grp % 2)
                    for t in range(TT):
                        dst = z_ps[lo_p:lo_p + 64, grp // 2, t * P:t * P + P]
                        mm(dst, ones_row[:], sbias[:, grp, :], start=True, stop=False)
                        last = mm(dst, v_z[:, t, 64 * grp:64 * grp + 64], wt[:, grp, :], start=False, stop=True)
                last.then_inc(z_done, 1)

            def sums_bc(l, c):
                pe.wait_ge(ysq_ready, l * 2 + c + 1)
                for t in range(TT):
                    for j in range(2):
                        last = mm(sumsq_bc[:, c, t, j, :], ysq[:, 2 * c + j, t * P:t * P + P], half_ones[:],
                                  start=True, stop=True)
                last.then_inc(sumbc_done, 1)

            def spread_bc(l, c):
                pe.wait_ge(rows_bc_ready, l * 2 + c + 1)
                if c == 0:
                    pe.wait_ge(cross_kept, l + 1)
                else:
                    pe.wait_ge(yc_ready, l + 1)
                for j in range(2):
                    for t in range(TT):
                        last = mm(spread_bc_ps[:, j, t * P:t * P + P], rows_bc[:, c, t, j, :], ident[:],
                                  start=True, stop=True)
                last.then_inc(spread_bc_done, 1)

            def outputs_a(l):
                pe.wait_ge(vals_ready, l * 4 + 4)
                pe.wait_ge(z_free[0], l * 6 + 6)
                pe.wait_ge(z_free[1], l * 6 + 6)
                pe.wait_ge(score_kept, l * 8 + 8)
                for h in range(HEADS):
                    v0, v1 = vals[:, 0, h * P:h * P + P], vals[:, 1, h * P:h * P + P]
                    mm(o_ps[:, h, 0:P], v0, scores[:, h * TT, :], start=True, stop=True)
                    mm(o_ps[:, h, P:2 * P], v0, cross[:, h, :], start=True, stop=False)
                    last = mm(o_ps[:, h, P:2 * P], v1, scores[:, h * TT + 1, :], start=False, stop=True)
                last.then_inc(o_done, 1)

            def sums_a(l):
                pe.wait_ge(osq_ready, l + 1)
                for t in range(TT):
                    for h in range(HEADS):
                        last = mm(sumsq_a[:, t, h:h + 1], osq[:, h, t * P:t * P + P], ones_col[:],
                                  start=True, stop=True)
                last.then_inc(suma_done, 1)

            def spread_a(l):
                pe.wait_ge(rows_a_ready, l + 1)
                pe.wait_ge(og_ready, l + 1)
                for h in range(HEADS):
                    for t in range(TT):
                        last = mm(spread_a_ps[:, h, t * P:t * P + P], rows_a[:, t, h, :], ident[:],
                                  start=True, stop=True)
                    if h % 2 == 1:
                        last.then_inc(spread_a_done, 1)

            def mixer(l, norm):
                for n in range(N_IN):
                    slot, dst = slot_mix(n), zb[n % 2]
                    if n == 0:
                        first_chunk(slot, use_mix(l, n), norm, dst)
                    else:
                        pe.wait_ge(lo_ready[slot], use_mix(l, n) + 2)
                        if n >= 2:
                            pe.wait_ge(z_free[n % 2], l * 6 + n // 2)
                        part = toks if n in (6, 7, 8) else cols
                        part(slot, dst, 0)
                        part(slot, dst, 1).then_inc(chunk_used[slot], 1)
                    if n >= 4:
                        score(l, n - 4)
                    if n == 6:
                        lru_gates(l)

                def out(c, tile, first, last, between=None):
                    j = N_IN + c
                    accumulate(slot_mix(j), use_mix(l, j), yhi[:, tile:tile + 2, :], ylo[:, tile:tile + 2, :],
                               first, last, between)

                sums_bc(l, 0)
                score(l, 8)
                spread_bc(l, 0)
                sgu_mix(l)
                outputs_a(l)
                sums_bc(l, 1)

                def small():
                    spread_bc(l, 1)
                    sums_a(l)

                pe.wait_ge(ylbc, l * 2 + 1)
                out(0, 4, True, False, small)
                spread_a(l)
                pe.wait_ge(ylbc, l * 2 + 2)
                out(1, 6, False, False)
                pe.wait_ge(yla, l * 2 + 1)
                out(2, 0, False, False)
                pe.wait_ge(yla, l * 2 + 2)
                out(3, 2, False, True)

            for slot in range(3):
                pe.sem_inc(chunk_used[slot], 1)
            pe.wait_ge(ones_made, 3)
            pe.wait_ge(ident_landed, 16)
            with pe.Fori(0, DEPTH) as l:
                swiglu(l, 0, l * 3)
                mixer(l, l * 3 + 1)
                swiglu(l, 1, l * 3 + 2)
            sum_squares(3 * DEPTH)
            spread_rinv(3 * DEPTH)

        @block.scalar
        def _(act):
            A = nc.scalar.activation
            act.dma_start(par_all[:], params).then_inc(par_landed, 16)
            act.dma_start(ident[:], identity).then_inc(ident_landed, 16)
            for dst, src in ((gain_fin[:], gain_out), (bc[:].rearrange("p h t -> p (h t)"), masks), (tri[:], causal)):
                act.dma_start(dst, src).then_inc(const_landed, 16)

            def hi(slot, use):
                act.wait_ge(landed[slot], use * 16 + 16)
                act.wait_ge(chunk_used[slot], use + 1)
                nc.scalar.copy(whi[slot][:], raw[slot][:]).then_inc(hi_ready[slot], 1)

            def hi_mix(l, j):
                hi(slot_mix(j), use_mix(l, j))

            def split_x(col, m):
                A(xhi[:, m, :], x[:, m, :], ACT.Copy, scale=par[:, col + m:col + m + 1]).then_inc(xhi_ready, 1)

            def swiglu(l, f):
                g, u, d = ROLES[f]
                done = l * (2 * FCH) + f * FCH

                def silu(i):
                    act.wait_ge(gsc_ready, done + i + 1)
                    A(gact[:], gsc[:], ACT.Silu).then_inc(gact_ready, 1)

                def round_act(i):
                    act.wait_ge(actf_ready, done + i + 1)
                    act.wait_ge(chunk_used[d], use_f(l, f, d, i) + 1)
                    nc.scalar.copy(ahi[:], act_f[:]).then_inc(ahi_ready, 1)

                nc.scalar.preload_act_table(ACT.Silu)
                with act.Fori(0, FCH - 1) as i:
                    hi(g, use_f(l, f, g, i + 1))
                    silu(i)
                    hi(u, use_f(l, f, u, i + 1))
                    round_act(i)
                    hi(d, use_f(l, f, d, i))
                hi(g, use_f(l, f, g, FCH))
                silu(FCH - 1)
                hi(u, use_f(l, f, u, FCH))
                act.wait_ge(actf_ready, done + FCH)
                nc.scalar.copy(ahi_last, act_f[:]).then_inc(ahi_ready, 1)
                if f == 0:
                    vectors(l)

            def vectors(l):
                lam, tmp = par[:, C_LAM:C_LAM + 2], vec[:, 0:2]
                A(tmp, lam, ACT.Abs).then_inc(vec_act, 1)
                A(vec[:, 2:4], lam, ACT.Relu, scale=-1.0).then_inc(vec_act, 1)
                act.wait_ge(vec_act, l * 5 + 1)
                A(tmp, tmp, ACT.Exp, scale=-1.0).then_inc(vec_act, 1)
                act.wait_ge(vec_dve, l * VEC_STEPS + 2)
                A(vec[:, 8:16], vec[:, 8:16], ACT.Exp).then_inc(vec_act, 1)
                act.wait_ge(vec_act, l * 5 + 3)
                A(tmp, tmp, ACT.Ln, bias=1.0).then_inc(vec_act, 1)

            def mixer(l):
                def exp_level(j):
                    act.wait_ge(dist_ready, l * 8 + j)
                    A(dist[j % 2][:], dist[j % 2][:], ACT.Exp).then_inc(exp_ready, 1)

                def vals_out(n):
                    act.wait_ge(chunk_used[slot_mix(n)], use_mix(l, n) + 2)
                    c = (n - 6) * CW
                    A(vals[:, 0, c:c + CW], zb[n % 2][:, 0, :], ACT.Copy, scale=rinv_tok[:, 0:1]).then_inc(vals_ready, 1)
                    A(vals[:, 1, c:c + CW], zb[n % 2][:, 1, :], ACT.Copy, scale=rinv_tok[:, 1:2])\
                        .then_inc(vals_ready, 1)
                    act.wait_ge(vals_ready, l * 4 + (2 * (n - 6) + 2))
                    act.sem_inc(z_free[n % 2], 1)

                for n in range(10):
                    hi_mix(l, n + 3)
                    if n in (0, 1):
                        act.wait_ge(f_evac, l * 2 + n + 1)
                        A(fz[:, 2 * n:2 * n + 2, :], fz[:, 2 * n:2 * n + 2, :], ACT.Sigmoid).then_inc(f_sig, 1)
                    if n == 2:
                        act.wait_ge(clamp_ready, l + 1)
                        A(fz[:], fz[:], ACT.Ln).then_inc(logf_ready, 1)
                    if n == 3:
                        act.wait_ge(q_evac, l * 2 + 2)
                        A(qs[:], qz[:], ACT.Sigmoid).then_inc(q_sig, 1)
                    if n == 4:
                        exp_level(1)
                        exp_level(2)
                    if n == 6:
                        vals_out(n)
                        nc.scalar.copy(cross[:].rearrange("p a t -> p (a t)"), bank(7)).then_inc(cross_kept, 1)
                    if n == 7:
                        act.wait_ge(vec_dve, (l + 1) * VEC_STEPS)
                        act.wait_ge(gates_done, l + 1)
                        for m in range(2):
                            A(rt[:, m, :], gate_ps[:, 0, m, :], ACT.Tanh, bias=par[:, C_HBA + m:C_HBA + m + 1],
                              scale=0.5).then_inc(rg_tanh, 1)
                            A(gt[:, m, :], gate_ps[:, 1, m, :], ACT.Tanh, bias=par[:, C_HBX + m:C_HBX + m + 1],
                              scale=0.5).then_inc(rg_tanh, 1)
                        vals_out(n)
                    if n == 8:
                        act.wait_ge(chunk_used[slot_mix(n)], use_mix(l, n) + 2)
                        for t in range(TT):
                            A(v_z[:, t, :], zb[n % 2][:, t, :], ACT.Copy, scale=rinv_tok[:, t:t + 1])\
                                .then_inc(v_evac, 1)
                        act.wait_ge(v_evac, l * 2 + 2)
                        act.sem_inc(z_free[n % 2], 1)
                    if 5 <= n:
                        exp_level(n - 2)
                    if n == 8:
                        for m in range(2):
                            c4 = par[:, C_C4 + m:C_C4 + m + 1]
                            A(dec[:, m, :], rt[:, m, :], ACT.Exp, bias=c4, scale=c4).then_inc(dec_ready, 1)
                        for m in range(2):
                            c4 = par[:, C_C4 + m:C_C4 + m + 1]
                            A(th[:, m, :], rt[:, m, :], ACT.Tanh, bias=c4, scale=c4).then_inc(th_ready, 1)
                exp_level(8)
                act.wait_ge(v_evac, l * 2 + 2)
                A(v_z[:], v_z[:], ACT.Gelu_apprx_tanh).then_inc(v_gelu, 1)
                act.wait_ge(gate_evac, l + 1)
                A(gate_z, gate_z, ACT.Gelu_apprx_tanh).then_inc(gate_gelu, 1)
                act.wait_ge(u_evac, l + 1)
                A(u_z, u_z, ACT.Gelu_apprx_tanh).then_inc(u_gelu, 1)
                act.wait_ge(mult2_ready, l + 1)
                A(rt[:], th[:], ACT.Sqrt, scale=-0.25).then_inc(mult_ready, 1)
                act.wait_ge(v_cent, l + 1)
                act.wait_ge(mult_ready, l + 1)
                nc.scalar.square(v_squares[:], v_z[:]).then_inc(v_sq, 1)
                hi_mix(l, 13)

                def squares_bc(c):
                    nc.scalar.square(ysq[:, 2 * c:2 * c + 2, :], y_bc[:, 2 * c:2 * c + 2, :]).then_inc(ysq_ready, 1)

                def rms_of_bc(c):
                    act.wait_ge(sumbc_done, l * 2 + c + 1)
                    A(inv_bc[:, c], sumsq_bc[:, c], ACT.Sqrt, bias=eps_col[:], scale=1.0 / 64).then_inc(rms_bc, 1)
                    act.wait_ge(inv_bc_ready, l * 2 + c + 1)
                    A(rows_bc[:, c].rearrange("p t j (g s) -> p (t j g) s", s=64),
                      inv_bc[:, c].rearrange("p t j g -> p (t j g)").unsqueeze(2).to_broadcast([P, 8, 64]),
                      ACT.Copy).then_inc(rows_bc_ready, 1)

                def round_bc(c):
                    act.wait_ge(nbc_ready, l * 4 + 2 * c + 2)
                    nc.scalar.copy(yhi[:, 4 + 2 * c:6 + 2 * c, :], y_bc[:, 2 * c:2 * c + 2, :]).then_inc(yhbc, 1)

                act.wait_ge(wq_ready, l * 8 + 8)
                act.wait_ge(yb_ready, l + 1)
                squares_bc(0)
                rms_of_bc(0)
                act.wait_ge(g_evac, l * 2 + 2)
                A(qs[:], gz[:], ACT.Sigmoid).then_inc(g_sig, 1)
                round_bc(0)
                act.wait_ge(yc_ready, l + 1)
                squares_bc(1)
                act.wait_ge(o_done, l + 1)
                nc.scalar.square(osq[:], o_ps).then_inc(osq_ready, 1)
                rms_of_bc(1)
                hi_mix(l, 14)
                round_bc(1)
                act.wait_ge(suma_done, l + 1)
                A(inv_a[:], sumsq_a, ACT.Sqrt, bias=eps_col[:], scale=1.0 / 128).then_inc(rms_a, 1)
                act.wait_ge(inv_a_ready, l + 1)
                A(rows_a.rearrange("p t h s -> p (t h) s"),
                  inv_a[:].rearrange("p t h -> p (t h)").unsqueeze(2).to_broadcast([P, TT * HEADS, P]), ACT.Copy)\
                    .then_inc(rows_a_ready, 1)
                for p in range(2):
                    act.wait_ge(na_ready, l * 2 + p + 1)
                    nc.scalar.copy(yhi[:, 2 * p:2 * p + 2, :], gz[:, 2 * p:2 * p + 2, :]).then_inc(yha, 1)
                hi_mix(l, 15)
                hi(ROLES[1][0], use_f(l, 1, ROLES[1][0], 0))

            hi(0, 0)
            with act.Fori(0, DEPTH) as l:
                act.wait_ge(par_ready, l + 1)
                for m in range(KT):
                    if m % 2 == 0:
                        act.wait_ge(x_ready, l * 12 + (m // 2 + 1))
                    split_x(C_N1, m)
                hi(1, use_f(l, 0, 1, 0))
                swiglu(l, 0)
                for m in range(KT):
                    if m % 2 == 0:
                        act.wait_ge(x_ready, l * 12 + (m // 2 + 5))
                    split_x(C_NM, m)
                hi_mix(l, 1)
                hi_mix(l, 2)
                mixer(l)
                hi(ROLES[1][1], use_f(l, 1, ROLES[1][1], 0))
                for m in range(KT):
                    if m % 2 == 0:
                        act.wait_ge(x_ready, l * 12 + (m // 2 + 9))
                    split_x(C_N2, m)
                swiglu(l, 1)

        @block.gpsimd
        def _(pool):
            G = nc.gpsimd

            def squares(norm):
                for b in range(4):
                    pool.wait_ge(x_ready, norm * 4 + (b + 1))
                    G.tensor_tensor(xsq[:, 2 * b:2 * b + 2, :], x[:, 2 * b:2 * b + 2, :], x[:, 2 * b:2 * b + 2, :],
                                    ALU.mult).then_inc(xsq_ready, 1)
                rsqrt_tok(norm)

            def rsqrt_tok(norm):
                pool.wait_ge(var_ready, norm + 1)
                G.tensor_tensor(rinv_tok[:], tokvar[:], neg_half[:, 0:TT], ALU.pow).then_inc(rtok_ready, 1)

            def distances(l, j):
                if j > 2:
                    pool.wait_ge(wq_ready, l * 8 + (j - 2))
                    pool.wait_ge(wk_ready, l * 8 + (j - 2))
                h = (128,) + HALVES
                h = h[j - 1]
                buf = dist[j % 2]
                if h == 128:
                    b = bc[:].rearrange("p h (c s) -> p h c s", s=SUB)
                    o = buf[:].rearrange("p h (c s) -> p h c s", s=SUB)

                    def end(c):
                        return b[:, :, c, SUB - 1:SUB].to_broadcast([P, HEADS, SUB])
                    G.tensor_tensor(o[:, :, 0, :], end(0), b[:, :, 0, :], ALU.subtract).then_inc(dist_part, 1)
                    G.tensor_tensor(o[:, :, 1, :], end(1), b[:, :, 1, :], ALU.subtract)
                    G.tensor_copy(o[:, :, 2, :], b[:, :, 2, :])
                    pool.wait_ge(dist_part, l + 1)
                    G.tensor_tensor(o[:, :, 0, :], o[:, :, 0, :], end(1), ALU.add)
                    G.tensor_tensor(o[:, :, 3, :], b[:, :, 3, :], end(2), ALU.add).then_inc(dist_ready, 1)
                    return
                b = bc[:].rearrange("p h (n two s) -> p (h n) two s", two=2, s=h)
                o = buf[:].rearrange("p h (n two s) -> p (h n) two s", two=2, s=h)
                end = b[:, :, 0, h - 1:h].to_broadcast([P, HEADS * SEQ // (2 * h), h])
                G.tensor_tensor(o[:, :, 0, :], end, b[:, :, 0, :], ALU.subtract)
                if h == SUB:
                    G.tensor_copy(o[:, :, 1, :], b[:, :, 1, :]).then_inc(dist_ready, 1)
                else:
                    G.tensor_tensor(o[:, :, 1, :], b[:, :, 1, :], end, ALU.subtract).then_inc(dist_ready, 1)

            def weigh_keys(l, j):
                h = ((128,) + HALVES)[j - 1]
                pool.wait_ge(exp_ready, l * 8 + j)
                if j > 2:
                    pool.wait_ge(score_done, l * 9 + (j - 1))
                sel = "p h (n two s) -> p (h n) two s"
                o, e, k = (t[:].rearrange(sel, two=2, s=h)[:, :, 0, :] for t in (wqk[j % 2], dist[j % 2], kk))
                G.tensor_tensor(o, e, k, ALU.mult).then_inc(wk_ready, 1)

            def mixer(l):
                pool.wait_ge(b_ready, l + 1)
                distances(l, 1)
                pool.wait_ge(q_sig, l + 1)
                G.tensor_tensor(qq[:], qz[:], qs[:], ALU.mult).then_inc(q_ready, 1)
                distances(l, 2)
                for j in range(1, 9):
                    weigh_keys(l, j)
                    if j == 6:
                        pool.wait_ge(dec_ready, l * 2 + 2)
                        G.tensor_tensor(dec_sq, dec[:], dec[:], ALU.mult).then_inc(dec2_ready, 1)
                    if j + 2 <= 8:
                        distances(l, j + 2)
                pool.wait_ge(v_mean, l + 1)
                mean = v_stat[:, 0:8].unsqueeze(2).to_broadcast([P, 8, 64])
                vg = v_z[:].rearrange("p t (g c) -> p (t g) c", c=64)
                G.tensor_tensor(vg, vg, mean, ALU.subtract).then_inc(v_cent, 1)
                pool.wait_ge(mult_ready, l + 1)
                pool.wait_ge(lin_part, l + 1)
                G.tensor_tensor(lin[:], lin[:], rt[:], ALU.mult).then_inc(lin_ready, 1)
                pool.wait_ge(v_var, l + 1)
                G.tensor_tensor(v_stat[:, 16:24], v_stat[:, 8:16], neg_half[:], ALU.pow).then_inc(v_rstd, 1)
                pool.wait_ge(v_rstd, l + 1)
                pool.wait_ge(v_sq, l + 1)
                rstd = v_stat[:, 16:24].unsqueeze(2).to_broadcast([P, 8, 64])
                G.tensor_tensor(vg, vg, rstd, ALU.mult).then_inc(v_ready, 1)
                pool.wait_ge(g_sig, l + 1)
                G.tensor_tensor(gz[:], qs[:], gz[:], ALU.mult).then_inc(gs_ready, 1)

            G.memset(reset[:], 1.0).then_inc(setup_pool, 1)
            G.memset(neg_half[:], -0.5).then_inc(setup_pool, 1)
            pool.wait_ge(setup_pool, 2)
            G.memset(reset[:].rearrange("p (n s) -> p n s", s=SUB)[:, :, 0:1], 0.0)
            G.memset(scores[:], 0.0).then_inc(setup_pool, 1)
            squares(0)
            pool.wait_ge(const_landed, 16 * N_CONST)
            G.tensor_copy(mask[:].rearrange("p a t -> p (a t)"), bc[:].rearrange("p h t -> p (h t)"))\
                .then_inc(setup_pool, 1)
            with pool.Fori(0, DEPTH) as l:
                squares(l * 3 + 1)
                mixer(l)
                squares(l * 3 + 2)
                squares(l * 3 + 3)

        @block.vector
        def _(dve):
            V = nc.vector

            def lo(slot, use):
                dve.wait_ge(hi_ready[slot], use + 1)
                V.tensor_tensor(wlo[slot][:], raw[slot][:], whi[slot][:].bitcast(F32), ALU.subtract)\
                    .then_inc(lo_ready[slot], 1)

            def lo_mix(l, j):
                lo(slot_mix(j), use_mix(l, j))

            def split_x(norm, col, m):
                dve.wait_ge(xhi_ready, norm * KT + m + 1)
                V.scalar_tensor_tensor(xlo[:, m, :], x[:, m, :], par[:, col + m:col + m + 1],
                                       xhi[:, m, :].bitcast(F32), ALU.mult, ALU.subtract).then_inc(xlo_ready, 1)

            def residual(update, b, factor):
                dve.wait_ge(acc_done, update * 4 + b + 1)
                V.scalar_tensor_tensor(x[:, 2 * b:2 * b + 2, :], acc[:, 2 * b:2 * b + 2, :], factor,
                                       x[:, 2 * b:2 * b + 2, :], ALU.mult, ALU.add).then_inc(x_ready, 1)

            def residual_and_split(update, norm, col, factor):
                residual(update, 0, factor)
                for b in range(1, 4):
                    residual(update, b, factor)
                    split_x(norm, col, 2 * b - 2)
                    split_x(norm, col, 2 * b - 1)
                split_x(norm, col, 6)
                split_x(norm, col, 7)

            def norm_stats(norm):
                dve.wait_ge(normsum_ready, norm + 1)
                V.tensor_scalar(tokvar[:], normsum, 1.0 / D, EPS, ALU.mult, ALU.add).then_inc(var_ready, 1)
                dve.wait_ge(rtok_ready, norm + 1)
                V.tensor_copy(rinv_rows[:], rinv_tok[:].unsqueeze(2).to_broadcast([P, TT, P])).then_inc(rrows_ready, 1)
                dve.wait_ge(rps_ready, norm + 1)
                V.tensor_copy(rinv[:], rinv_ps).then_inc(rinv_ready, 1)

            logits = par_all[:, :, C_LBL:C_LBL + 4]
            top = vec[:, 4:8]
            vec_e = vec[:, 8:16].rearrange("p (l c) -> p l c", l=DEPTH)
            vec_b = vec[:, 16:24].rearrange("p (l c) -> p l c", l=DEPTH)

            def vec_step(l, n, ins):
                ins.then_inc(vec_dve, 1)
                dve.wait_ge(vec_dve, l * VEC_STEPS + n)

            def vectors_before(l):
                vec_step(l, 1, V.tensor_tensor(top, logits[:, 0, :], logits[:, 1, :], ALU.max))
                V.tensor_tensor(vec_e, logits, top.unsqueeze(1).to_broadcast([P, DEPTH, 4]), ALU.subtract)\
                    .then_inc(vec_dve, 1)
                V.tensor_scalar(par[:, C_HBA:C_HBA + 4], par[:, C_BA:C_BA + 4], 0.5, None, ALU.mult)

            def vectors_after(l):
                dve.wait_ge(vec_act, l * 5 + 4)
                vec_step(l, 3, V.tensor_tensor(top, vec_e[:, 0, :], vec_e[:, 1, :], ALU.add))
                vec_step(l, 4, V.reciprocal(top, top))
                vec_step(l, 5, V.tensor_tensor(vec_e, vec_e, top.unsqueeze(1).to_broadcast([P, DEPTH, 4]), ALU.mult))
                V.tensor_tensor(vec_b[:, 0, :], vec_e[:, 0, :], vec_e[:, 0, :], ALU.subtract)
                vec_step(l, 6, V.tensor_tensor(top, vec_e[:, 0, :], vec_e[:, 1, :], ALU.add))
                vec_step(l, 7, V.tensor_tensor(vec_b[:, 1, :], top, vec_e[:, 0, :], ALU.subtract))
                vec_step(l, 8, V.tensor_copy(par[:, C_LB:C_LB + 4],
                                             vec_b[:, ds(l, 1), :].rearrange("p a c -> p (a c)")))
                V.tensor_scalar(par[:, C_OML:C_OML + 4], par[:, C_LB:C_LB + 4], -1.0, 1.0, ALU.mult, ALU.add)
                dve.wait_ge(vec_act, l * 5 + 5)
                c4 = par[:, C_C4:C_C4 + 2]
                vec_step(l, 9, V.tensor_tensor(c4, vec[:, 0:2], vec[:, 2:4], ALU.add))
                V.tensor_scalar(c4, c4, -4.0, None, ALU.mult).then_inc(vec_dve, 1)

            rinv2 = rinv[:].unsqueeze(1).to_broadcast([P, 2, SEQ])

            def swiglu(l, f, norm):
                g, u, d = ROLES[f]
                done = l * (2 * FCH) + f * FCH

                def gate(i):
                    dve.wait_ge(rinv_ready, norm + 1)
                    dve.wait_ge(chunk_used[g], use_f(l, f, g, i) + 2)
                    V.tensor_tensor(gsc[:], zb[0], rinv2, ALU.mult).then_inc(gsc_ready, 1)

                def gated(i):
                    dve.wait_ge(chunk_used[u], use_f(l, f, u, i) + 2)
                    dve.wait_ge(gact_ready, done + i + 1)
                    V.tensor_tensor(up[:], zb[1], gact[:], ALU.mult).then_inc(up_ready, 1)
                    dve.wait_ge(up_ready, done + i + 1)
                    V.tensor_tensor(act_f[:], up[:], rinv2, ALU.mult).then_inc(actf_ready, 1)

                def split_act(i):
                    dve.wait_ge(ahi_ready, done + i + 1)
                    V.tensor_tensor(alo[:], act_f[:], ahi[:].bitcast(F32), ALU.subtract).then_inc(alo_ready, 1)

                norm_stats(norm)
                if f == 0:
                    vectors_before(l)
                with dve.Fori(0, FCH - 1) as i:
                    gate(i)
                    lo(g, use_f(l, f, g, i + 1))
                    gated(i)
                    lo(u, use_f(l, f, u, i + 1))
                    split_act(i)
                    lo(d, use_f(l, f, d, i))
                gate(FCH - 1)
                lo(g, use_f(l, f, g, FCH))
                gated(FCH - 1)
                dve.wait_ge(ahi_ready, done + FCH)
                V.tensor_tensor(alo_last, act_f[:], ahi_last.bitcast(F32), ALU.subtract).then_inc(alo_ready, 1)
                lo(u, use_f(l, f, u, FCH))
                if f == 0:
                    vectors_after(l)

            def mixer(l, norm):
                def evac(n, dst, signal):
                    dve.wait_ge(rinv_ready, norm + 1)
                    dve.wait_ge(chunk_used[slot_mix(n)], use_mix(l, n) + 2)
                    V.tensor_tensor(dst, zb[n % 2], rinv2, ALU.mult).then_inc(signal, 1)

                def freed(n, signal, value):
                    dve.wait_ge(signal, value)
                    dve.sem_inc(z_free[n % 2], 1)

                def weigh_queries(j):
                    h = ((128,) + HALVES)[j - 1]
                    dve.wait_ge(exp_ready, l * 8 + j)
                    dve.wait_ge(q_ready, l + 1)
                    if j > 2:
                        dve.wait_ge(score_done, l * 9 + (j - 1))
                    sel = "p h (n two s) -> p (h n) two s"
                    o, e, q = (t[:].rearrange(sel, two=2, s=h)[:, :, 1, :] for t in (wqk[j % 2], dist[j % 2], qq))
                    V.tensor_tensor(o, e, q, ALU.mult).then_inc(wq_ready, 1)

                def keep(j):
                    kept = 0 if j == 0 else j - 1
                    which = len(HALVES) if j == 0 else j - 2
                    dve.wait_ge(score_done, l * 9 + j + 1)
                    dve.sem_inc(keep_begun, 1)
                    m = mask[:, which, :].unsqueeze(1).to_broadcast([P, HEADS * TT, P])
                    V.copy_predicated(scores[:], m, sc_ps[j // 8]).then_inc(score_kept, 1)
                    dve.wait_ge(score_kept, l * 8 + kept + 1)

                def conv():
                    for m in range(2):
                        V.tensor_scalar(xc[:, m, :], xpad[:, m, 0:SEQ], par[:, C_CW + m:C_CW + m + 1],
                                        par[:, C_CB + m:C_CB + m + 1], ALU.mult, ALU.add).then_inc(conv_step, 1)
                    for tap in range(1, 4):
                        dve.wait_ge(conv_step, l * 6 + 2 * tap)
                        for m in range(2):
                            c = C_CW + 2 * tap + m
                            V.scalar_tensor_tensor(xc[:, m, :], xpad[:, m, tap:tap + SEQ], par[:, c:c + 1],
                                                   xc[:, m, :], ALU.mult, ALU.add)\
                                .then_inc(conv_step if tap < 3 else xc_ready, 1)

                vg = v_z[:].rearrange("p t (g c) -> p (t g) c", c=64)

                def step(n):
                    if n in (0, 1):
                        evac(n, fz[:, 2 * n:2 * n + 2, :], f_evac)
                        freed(n, f_evac, l * 2 + n + 1)
                    if n in (2, 3):
                        evac(n, qz[:, 2 * n - 4:2 * n - 2, :], q_evac)
                        freed(n, q_evac, l * 2 + (n - 1))
                    if n == 4:
                        evac(n, xpad[:, :, 3:3 + SEQ], xb_evac)
                        freed(n, xb_evac, l + 1)
                    if n == 5:
                        evac(n, gate_z, gate_evac)
                        freed(n, gate_evac, l + 1)
                    if n == 9:
                        evac(n, u_z, u_evac)
                        freed(n, u_evac, l + 1)
                    if n in (10, 11):
                        evac(n, gz[:, 2 * n - 20:2 * n - 18, :], g_evac)
                        freed(n, g_evac, l * 2 + (n - 9))
                    if n == 11:
                        return
                    if 5 <= n <= 9:
                        weigh_queries(n - 3)
                    if n == 10:
                        return
                    lo_mix(l, n + 3)
                    if n == 1:
                        dve.wait_ge(f_sig, l * 2 + 2)
                        for h in range(HEADS):
                            V.tensor_scalar(fz[:, h, :], fz[:, h, :], par[:, C_OML + h:C_OML + h + 1],
                                            par[:, C_LB + h:C_LB + h + 1], ALU.mult, ALU.add).then_inc(forget_ready, 1)
                        dve.wait_ge(forget_ready, l * 4 + 4)
                        V.tensor_scalar(kk[:], fz[:], -1.0, 1.0, ALU.mult, ALU.add).then_inc(k_ready, 1)
                        dve.wait_ge(k_ready, l + 1)
                        V.tensor_scalar(fz[:], fz[:], 2.0 ** -63, None, ALU.max).then_inc(clamp_ready, 1)
                    if n == 2:
                        dve.wait_ge(logf_ready, l + 1)
                        V.tensor_tensor_scan(bc[:].rearrange("p h t -> p (h t)"), reset[:],
                                             fz[:].rearrange("p h t -> p (h t)"), 0.0, ALU.mult, ALU.add)\
                            .then_inc(b_ready, 1)
                    if n == 4:
                        weigh_queries(1)
                        keep(0)
                    if 6 <= n <= 9:
                        keep(n - 4)
                    if n == 5:
                        conv()
                    if n == 8:
                        dve.wait_ge(rg_tanh, l * 4 + 4)
                        V.scalar_tensor_tensor(lin[:], gt[:], 1.0, xc[:], ALU.add, ALU.mult).then_inc(lin_part, 1)
                    if n == 9:
                        dve.wait_ge(dec2_ready, l + 1)
                        dve.wait_ge(th_ready, l * 2 + 2)
                        V.scalar_tensor_tensor(th[:], dec_sq, 1.0, th[:], ALU.add, ALU.mult)\
                            .then_inc(mult2_ready, 1)

                lo_mix(l, 2)
                dve.wait_ge(setup_pool, 4)
                dve.wait_ge(small_landed, l * 48 + 48)
                V.tensor_tensor(wt[:], wt[:], tri[:].unsqueeze(1).to_broadcast([P, 4, P]), ALU.mult)\
                    .then_inc(wt_masked, 1)
                norm_stats(norm)
                for n in range(10):
                    step(n)
                weigh_queries(7)
                dve.wait_ge(v_gelu, l + 1)
                V.reduce_sum(v_stat[:, 0:8], vg, AX.X).then_inc(v_part, 1)
                dve.wait_ge(v_part, l * 2 + 1)
                V.tensor_scalar(v_stat[:, 0:8], v_stat[:, 0:8], 1.0 / 64, None, ALU.mult).then_inc(v_mean, 1)
                step(10)
                dve.wait_ge(v_sq, l + 1)
                V.reduce_sum(v_stat[:, 8:16], v_squares[:].rearrange("p j (g c) -> p (j g) c", c=64), AX.X)\
                    .then_inc(v_part, 1)
                dve.wait_ge(v_part, l * 2 + 2)
                V.tensor_scalar(v_stat[:, 8:16], v_stat[:, 8:16], 1.0 / 64, EPS, ALU.mult, ALU.add)\
                    .then_inc(v_var, 1)
                keep(6)
                weigh_queries(8)
                dve.wait_ge(lin_ready, l + 1)
                for m in range(2):
                    V.tensor_tensor_scan(xc[:, m, :], dec[:, m, :], lin[:, m, :], 0.0, ALU.mult, ALU.add)\
                        .then_inc(h_ready, 1)
                dve.wait_ge(h_ready, l * 2 + 2)
                dve.wait_ge(gate_gelu, l + 1)
                V.tensor_tensor(y_bc[:, 0:2, :], xc[:], gate_z, ALU.mult).then_inc(yb_ready, 1)
                step(11)
                keep(7)

                def inverse_bc(c):
                    dve.wait_ge(rms_bc, l * 2 + c + 1)
                    V.reciprocal(inv_bc[:, c], inv_bc[:, c]).then_inc(inv_bc_ready, 1)

                def normalise_bc(c):
                    dve.wait_ge(spread_bc_done, l * 2 + c + 1)
                    for j in range(2):
                        y, gain = y_bc[:, 2 * c + j, :], par[:, C_GBC + 2 * c + j:C_GBC + 2 * c + j + 1]
                        V.scalar_tensor_tensor(y, y, gain, spread_bc_ps[:, j, :], ALU.mult, ALU.mult)\
                            .then_inc(nbc_ready, 1)

                def split_bc(c):
                    o = slice(4 + 2 * c, 6 + 2 * c)
                    dve.wait_ge(yhbc, l * 2 + c + 1)
                    V.tensor_tensor(ylo[:, o, :], y_bc[:, 2 * c:2 * c + 2, :], yhi[:, o, :].bitcast(F32), ALU.subtract)\
                        .then_inc(ylbc, 1)

                inverse_bc(0)
                keep(8)
                normalise_bc(0)
                split_bc(0)
                dve.wait_ge(u_gelu, l + 1)
                dve.wait_ge(z_done, l + 1)
                V.tensor_tensor(y_bc[:, 2:4, :], z_ps, u_z, ALU.mult).then_inc(yc_ready, 1)
                lo_mix(l, 13)
                inverse_bc(1)
                dve.wait_ge(osq_ready, l + 1)
                dve.wait_ge(gs_ready, l + 1)
                for h in range(HEADS):
                    ins = V.scalar_tensor_tensor(gz[:, h, :], o_ps[:, h, :], par[:, C_HN + h:C_HN + h + 1],
                                                 gz[:, h, :], ALU.mult, ALU.mult)
                ins.then_inc(og_ready, 1)
                normalise_bc(1)
                split_bc(1)
                dve.wait_ge(rms_a, l + 1)
                V.reciprocal(inv_a[:], inv_a[:]).then_inc(inv_a_ready, 1)
                lo_mix(l, 14)
                dve.wait_ge(og_ready, l + 1)
                for p in range(2):
                    o = slice(2 * p, 2 * p + 2)
                    dve.wait_ge(spread_a_done, l * 2 + p + 1)
                    V.tensor_tensor(gz[:, o, :], spread_a_ps[:, o, :], gz[:, o, :], ALU.mult).then_inc(na_ready, 1)
                for p in range(2):
                    o = slice(2 * p, 2 * p + 2)
                    dve.wait_ge(yha, l * 2 + p + 1)
                    V.tensor_tensor(ylo[:, o, :], gz[:, o, :], yhi[:, o, :].bitcast(F32), ALU.subtract)\
                        .then_inc(yla, 1)
                lo_mix(l, N_MIX - 1)
                lo(ROLES[1][0], use_f(l, 1, ROLES[1][0], 0))

            for slot in range(3):
                dve.sem_inc(lo_ready[slot], 1)
            V.memset(ones_col[:], 1.0).then_inc(ones_made, 1)
            V.memset(ones_row[:], 1.0)
            V.memset(xpad[:, :, 0:3], 0.0)
            V.memset(eps_col[:], EPS)
            V.memset(half_ones[0:64, 0:1], 1.0)
            V.memset(half_ones[64:128, 0:1], 0.0)
            V.memset(half_ones[0:64, 1:2], 0.0).then_inc(ones_made, 1)
            V.memset(half_ones[64:128, 1:2], 1.0).then_inc(ones_made, 1)
            lo(0, 0)
            dve.wait_ge(par_landed, 16)
            dve.wait_ge(x_landed, 16)
            dve.sem_inc(x_ready, 4)
            with dve.Fori(0, DEPTH) as l:
                V.tensor_copy(par[:, 0:N_PAR], par_all[:, ds(l, 1), :].rearrange("p a c -> p (a c)")).then_inc(par_ready, 1)
                dve.wait_ge(par_ready, l + 1)
                for m in range(KT):
                    split_x(l * 3, C_N1, m)
                lo(1, use_f(l, 0, 1, 0))
                swiglu(l, 0, l * 3)
                residual_and_split(l * 3, l * 3 + 1, C_NM, 0.5)
                lo_mix(l, 1)
                mixer(l, l * 3 + 1)
                residual_and_split(l * 3 + 1, l * 3 + 2, C_N2, 1.0)
                lo(ROLES[1][1], use_f(l, 1, ROLES[1][1], 0))
                swiglu(l, 1, l * 3 + 2)
                for b in range(4):
                    residual(l * 3 + 2, b, 0.5)
            norm_stats(3 * DEPTH)
            dve.wait_ge(rinv_ready, 3 * DEPTH + 1)
            for m in range(KT):
                ins = V.scalar_tensor_tensor(xsq[:, m, :], x[:, m, :], gain_fin[:, m:m + 1], rinv[:],
                                             ALU.mult, ALU.mult)
                if m % 4 == 3:
                    ins.then_inc(outt_ready, 1)


def chunks_of_columns(w, order=None):
    n = w.shape[1] // CW
    c = w.reshape(KT, P, n, CW).transpose(2, 1, 0, 3).reshape(n, P, CHUNK)
    return c if order is None else c[list(order)]


def chunks_of_rows(w, order=None):
    n = w.shape[0] // (2 * P)
    c = w.reshape(n, 2, P, D).transpose(0, 2, 1, 3).reshape(n, P, CHUNK)
    return c if order is None else c[list(order)]


def swiglu_chunks(wg, wu, wd):
    g, u, d = chunks_of_columns(wg), chunks_of_columns(wu), chunks_of_rows(wd)
    out = [g[0], u[0]]
    for i in range(1, FCH):
        out += [g[i], u[i], d[i - 1]]
    return out + [d[FCH - 1]]


def kernel(**inputs):
    import concourse.bacc as bacc
    from concourse import mybir
    from concourse.bass_utils import run_bass_kernel_spmd

    a = {k: np.asarray(v) for k, v in inputs.items()}
    f32 = np.float32
    stream = np.zeros((DEPTH * PER_LAYER + 1, P, CHUNK), f32)
    at = 0
    for l in range(DEPTH):
        parts = swiglu_chunks(a["ffn1_wg"][l], a["ffn1_wu"][l], a["ffn1_wd"][l])
        parts += list(chunks_of_columns(a["w_in"][l], IN_ORDER)) + list(chunks_of_rows(a["w_out"][l], OUT_ORDER))
        parts += swiglu_chunks(a["ffn2_wg"][l], a["ffn2_wu"][l], a["ffn2_wd"][l])
        for part in parts:
            stream[at] = part
            at += 1

    def tiles(v):
        return v.reshape(-1, P).T

    params = np.zeros((P, DEPTH, N_PAR), f32)
    bd = np.zeros((P, DEPTH, 4, P), f32)
    for l in range(DEPTH):
        for c, v in ((C_N1, a["ffn1_norm"]), (C_NM, a["mix_norm"]), (C_N2, a["ffn2_norm"]), (C_HN, a["hgrn_norm"]),
                     (C_CW, a["conv_w"]), (C_CB, a["conv_b"]), (C_BA, a["lru_ba"]), (C_BX, a["lru_bx"]),
                     (C_LAM, a["lru_lambda"]), (C_GBC, a["lru_norm"]), (C_GBC + 2, a["sgu_norm"]),
                     (C_LBL, a["hgrn_lb_logits"])):
            t = tiles(v[l])
            params[:, l, c:c + t.shape[1]] = t
        for which, w in enumerate((a["lru_wa"], a["lru_wx"])):
            for blk in range(4):
                o = 64 * (blk % 2)
                bd[o:o + 64, l, 2 * which + blk // 2, o:o + 64] = w[l, blk]
    s = np.arange(P)[:, None]
    t = np.arange(P)[None, :]
    masks = np.zeros((P, len(HALVES) + 1, P), f32)
    for n, h in enumerate(HALVES):
        masks[:, n] = (s // (2 * h) == t // (2 * h)) & (s % (2 * h) < h) & (t % (2 * h) >= h)
    masks[:, -1] = s == t
    arrays = {
        "x_t": np.ascontiguousarray(a["x"][0].T.reshape(KT, P, SEQ).transpose(1, 0, 2)),
        "wstream": stream,
        "params": params,
        "gain_out": np.ascontiguousarray(tiles(a["final_norm"])),
        "block_diag": bd.reshape(P, DEPTH, 4 * P),
        "sgu_wt": np.ascontiguousarray(a["sgu_w"].transpose(3, 0, 1, 2)).reshape(P, DEPTH, 4 * P),
        "sgu_bias": np.ascontiguousarray(a["sgu_b"]).reshape(1, DEPTH, 4 * P),
        "identity": np.eye(P, dtype=f32),
        "masks": masks.reshape(P, -1),
        "causal": (s <= t).astype(f32),
    }
    nc = bacc.Bacc("TRN2", target_bir_lowering=False, num_devices=1)
    args = [nc.dram_tensor(k, v.shape, mybir.dt.from_np(v.dtype), kind="ExternalInput").ap()
            for k, v in arrays.items()]
    out = nc.dram_tensor("out_t", (P, KT, SEQ), mybir.dt.float32, kind="ExternalOutput").ap()
    build(nc, *args, out)
    got = run_bass_kernel_spmd(nc, [arrays], core_ids=[0]).results[0]["out_t"]
    return np.ascontiguousarray(got.transpose(1, 0, 2).reshape(D, SEQ).T)[None]
```

```python
import numpy as np

DEPTH, D, SEQ, DFF = 2, 1024, 256, 2816
P = 128
KT = D // P
TT = SEQ // P
CW = 256
CHUNK = KT * CW
FCH = DFF // CW
HEADS = 4
DA, DB, DC = 512, 256, 256
SUB = 64
EPS = 1e-6
N_IN, N_OUT = 12, 4
PER_LAYER = 2 * 3 * FCH + N_IN + N_OUT
IN_ORDER = (2, 3, 0, 1, 8, 9, 4, 5, 11, 10, 6, 7)
OUT_ORDER = (2, 3, 0, 1)
HALVES = (64, 32, 16, 8, 4, 2, 1)

C_N1, C_NM, C_N2, C_HN, C_CW, C_CB, C_BA, C_BX, C_LAM, C_GBC, C_LBL = 0, 8, 16, 24, 28, 36, 38, 40, 42, 44, 48
N_PAR = 52
C_LB, C_OML, C_C4, C_HBA, C_HBX = 52, 56, 60, 62, 64
N_ALL = 66
N_MASK = len(HALVES) * P // 2 + P
N_CONST = 2
SUM_AT, SPREAD_AT = 3, 2
VEC_STEPS = 10


def build(nc, x_in, wstream, params, block_diag, sgu_wt, sgu_bias, group_rows, identity, masks, causal, out):
    import concourse.bass as bass
    from concourse import mybir
    from contextlib import ExitStack

    F32, F32R, U8 = mybir.dt.float32, mybir.dt.float32r, mybir.dt.uint8
    ALU, ACT, AX = mybir.AluOpType, mybir.ActivationFunctionType, mybir.AxisListType
    ds = bass.ds

    with ExitStack() as ctx:
        def sb(name, shape, dt=F32):
            return ctx.enter_context(nc.sbuf_tensor(name, shape, dt))

        def sem(name):
            return ctx.enter_context(nc.semaphore(name))

        raw = [sb(f"raw{s}", [P, CHUNK]) for s in range(3)]
        whi = [sb(f"whi{s}", [P, CHUNK], F32R) for s in range(3)]
        wlo = [sb(f"wlo{s}", [P, CHUNK], F32R) for s in range(3)]
        x = sb("x", [P, KT, SEQ])
        xhi = sb("xhi", [P, KT, SEQ], F32R)
        xlo = sb("xlo", [P, KT, SEQ], F32R)
        yhi = sb("yhi", [P, KT, SEQ], F32R)
        ylo = sb("ylo", [P, KT, SEQ], F32R)
        xsq = sb("xsq", [P, KT, SEQ])
        rinv = sb("rinv", [P, SEQ])
        rinv_tok = sb("rinv_tok", [P, TT])
        tokvar = sb("tokvar", [P, TT])
        rinv_rows = sb("rinv_rows", [P, TT, P])
        par_all = sb("par_all", [P, DEPTH + 1, N_PAR])
        par = sb("par", [P, N_ALL])
        vec = sb("vec", [P, 24])
        bd = sb("bd", [P, 4, P])
        wt = sb("wt", [P, 4, P])
        tri = sb("tri", [P, P])
        sbias = sb("sbias", [4, TT, P])
        group_of = sb("group_of", [4, 2, P])
        ident = sb("ident", [P, P])
        mask = sb("mask", [P, N_MASK], U8)
        ones_col = sb("ones_col", [P, 1])
        half_ones = sb("half_ones", [P, 2])
        eps_col = sb("eps_col", [P, 1])
        reset = sb("reset", [P, HEADS * SEQ])
        neg_half = sb("neg_half", [P, 8])
        ahi = sb("ahi", [P, 2, SEQ], F32R)
        alo = sb("alo", [P, 2, SEQ], F32R)
        ahi_last, alo_last = yhi[:, 0:2, :], ylo[:, 0:2, :]
        fz = sb("fz", [P, HEADS, SEQ])
        kk = sb("kk", [P, HEADS, SEQ])
        qz = sb("qz", [P, HEADS, SEQ])
        qs = sb("qs", [P, HEADS, SEQ])
        qq = sb("qq", [P, HEADS, SEQ])
        bc = sb("bc", [P, HEADS, SEQ])
        dist = [sb(f"dist{i}", [P, HEADS, SEQ]) for i in range(2)]
        wqk = [sb(f"wqk{i}", [P, HEADS, SEQ]) for i in range(2)]
        scores = sb("scores", [P, HEADS * TT, P])
        cross = sb("cross", [P, HEADS, P])
        vals = sb("vals", [P, TT, DA])
        gz = fz
        osq = kk
        gate_z, u_z = qz[:, 0:2, :], qz[:, 2:4, :]
        inv_a = sb("inv_a", [P, TT, HEADS])
        inv_bc = sb("inv_bc", [P, 2, TT, 2, 2])
        rows_bc = dist[1][:].rearrange("p (c t) (j s) -> p c t j s", c=2, s=P)
        rows_a = dist[0][:].rearrange("p (t a) (b s) -> p t (a b) s", t=TT, s=P)
        xpad = sb("xpad", [P, 2, 3 + SEQ])
        xc = sb("xc", [P, 2, SEQ])
        rt = sb("rt", [P, 2, SEQ])
        gt = sb("gt", [P, 2, SEQ])
        th = sb("th", [P, 2, SEQ])
        dec = sb("dec", [P, 2, SEQ])
        lin = sb("lin", [P, 2, SEQ])
        v_z = sb("v_z", [P, TT, DC])
        v_stat = sb("v_stat", [P, 24])
        xg = (qs, kk)
        y_bc = bc
        ysq = (gt, lin)
        dec_sq = xsq[:, 0:2, :]
        v_squares = th
        gsc, gact, up, act_f = rt, gt, th, dec

        ps = ctx.enter_context(nc.psum_tensor("ps", [P, 8 * 512], F32))

        def bank(b, n=1):
            return ps[:, 512 * b:512 * (b + n)]

        acc = bank(0, 4).rearrange("p (m t) -> p m t", t=SEQ)
        zb = [bank(4).rearrange("p (m t) -> p m t", t=SEQ), bank(5).rearrange("p (m t) -> p m t", t=SEQ)]
        normsum = ps[:, 6 * 512:6 * 512 + TT]
        rinv_ps = ps[:, 6 * 512 + 256:7 * 512]
        diag_ps = bank(0, 2).rearrange("p (a t) -> p a t", t=P)
        cross_ps = bank(7).rearrange("p (a t) -> p a t", t=P)
        gate_ps = bank(2, 2).rearrange("p (a m t) -> p a m t", a=2, t=SEQ)
        o_ps = bank(4, 2).rearrange("p (h t) -> p h t", t=SEQ)
        z_ps = bank(7).rearrange("p (j t) -> p j t", t=SEQ)
        sumsq_bc = ps[:, 6 * 512 + 8:6 * 512 + 24].rearrange("p (c t j s) -> p c t j s", c=2, t=TT, j=2)
        sumsq_a = ps[:, 6 * 512 + 24:6 * 512 + 32].rearrange("p (t h) -> p t h", t=TT)
        spread_bc_ps = [bank(b).rearrange("p (j t) -> p j t", t=SEQ) for b in (2, 7)]
        spread_a_ps = o_ps

        const_landed, x_landed, out_landed = sem("const_landed"), sem("x_landed"), sem("out_landed")
        v_part = sem("v_part")
        ident_landed, par_landed = sem("ident_landed"), sem("par_landed")
        group_landed = sem("group_landed")
        small_landed, wt_masked = sem("small_landed"), sem("wt_masked")
        landed = [sem(f"landed{s}") for s in range(3)]
        hi_ready = [sem(f"hi_ready{s}") for s in range(3)]
        lo_ready = [sem(f"lo_ready{s}") for s in range(3)]
        chunk_used = [sem(f"chunk_used{s}") for s in range(3)]
        ones_made, setup_pool = sem("ones_made"), sem("setup_pool")
        par_ready = sem("par_ready")
        vec_act, vec_dve = sem("vec_act"), sem("vec_dve")
        x_ready = sem("x_ready")
        xhi_ready, xlo_ready = sem("xhi_ready"), sem("xlo_ready")
        xsq_pool, xsq_act, xsq_sum = sem("xsq_pool"), sem("xsq_act"), sem("xsq_sum")
        normsum_ready, var_ready, rtok_ready = sem("normsum_ready"), sem("var_ready"), sem("rtok_ready")
        rrows_ready, rps_ready, rinv_ready = sem("rrows_ready"), sem("rps_ready"), sem("rinv_ready")
        gsc_ready, gact_ready, up_ready = sem("gsc_ready"), sem("gact_ready"), sem("up_ready")
        actf_ready, ahi_ready, alo_ready = sem("actf_ready"), sem("ahi_ready"), sem("alo_ready")
        acc_done = sem("acc_done")
        z_free = [sem("z_free0"), sem("z_free1")]
        f_evac, f_sig, forget_ready, k_ready, clamp_ready = (
            sem("f_evac"), sem("f_sig"), sem("forget_ready"), sem("k_ready"), sem("clamp_ready"))
        logf_ready, b_ready = sem("logf_ready"), sem("b_ready")
        q_evac, q_sig, q_ready = sem("q_evac"), sem("q_sig"), sem("q_ready")
        dist_part = sem("dist_part")
        dist_ready, exp_ready = sem("dist_ready"), sem("exp_ready")
        wq_ready, wk_ready = sem("wq_ready"), sem("wk_ready")
        score_done, score_kept = sem("score_done"), sem("score_kept")
        cross_kept, keep_begun = sem("cross_kept"), sem("keep_begun")
        vals_ready = sem("vals_ready")
        xb_evac, conv_step, xc_ready = sem("xb_evac"), sem("conv_step"), sem("xc_ready")
        gates_done, rg_tanh, th_ready = sem("gates_done"), sem("rg_tanh"), sem("th_ready")
        dec_ready, dec2_ready, mult2_ready, mult_ready = (
            sem("dec_ready"), sem("dec2_ready"), sem("mult2_ready"), sem("mult_ready"))
        lin_part, lin_ready, h_ready, yb_ready = sem("lin_part"), sem("lin_ready"), sem("h_ready"), sem("yb_ready")
        gate_evac, gate_gelu, u_evac, u_gelu = sem("gate_evac"), sem("gate_gelu"), sem("u_evac"), sem("u_gelu")
        v_evac, v_gelu, v_mean, v_cent, v_sq, v_var, v_rstd, v_ready = (
            sem("v_evac"), sem("v_gelu"), sem("v_mean"), sem("v_cent"), sem("v_sq"), sem("v_var"),
            sem("v_rstd"), sem("v_ready"))
        z_done, yc_ready = sem("z_done"), sem("yc_ready")
        ysq_ready, sumbc_done = sem("ysq_ready"), sem("sumbc_done")
        rms_bc, inv_bc_ready, nbc_ready = sem("rms_bc"), sem("inv_bc_ready"), sem("nbc_ready")
        rows_bc_ready, spread_bc_done = sem("rows_bc_ready"), sem("spread_bc_done")
        rows_a_ready, spread_a_done = sem("rows_a_ready"), sem("spread_a_done")
        yhbc, ylbc = sem("yhbc"), sem("ylbc")
        g_evac, g_sig, gs_ready = sem("g_evac"), sem("g_sig"), sem("gs_ready")
        o_done, osq_ready, og_ready = sem("o_done"), sem("osq_ready"), sem("og_ready")
        suma_done, rms_a, inv_a_ready = sem("suma_done"), sem("rms_a"), sem("inv_a_ready")
        na_ready, yha, yla = sem("na_ready"), sem("yha"), sem("yla")
        xg_ready = sem("xg_ready")
        out_ready = sem("out_ready")

        ROLES = ((0, 1, 2), (2, 0, 1))
        USED_F = (FCH + 1, FCH, FCH - 1)
        N_MIX = N_IN + N_OUT
        USED_MIX = [len(range((s - 1) % 3, N_MIX, 3)) for s in range(3)]
        USES = [USED_F[s] + USED_MIX[s] + USED_F[ROLES[1].index(s)] for s in range(3)]

        def use_f(l, f, slot, i):
            return l * USES[slot] + (i + f * (USED_F[slot] + USED_MIX[slot]))

        def slot_mix(j):
            return (j + 1) % 3

        def use_mix(l, j):
            return l * USES[slot_mix(j)] + (USED_F[slot_mix(j)] + j // 3)


        block = ctx.enter_context(nc.Block())

        @block.sync
        def _(sp):
            def load(slot, use, chunk):
                sp.wait_ge(lo_ready[slot], use + 1)
                sp.dma_start(raw[slot][:], wstream[ds(chunk, 1)].rearrange("a p c -> p (a c)"))\
                    .then_inc(landed[slot], 16)

            def load_swiglu(l, f, first):
                g, u, d = ROLES[f]
                load(u, use_f(l, f, u, 0), first + 1)
                with sp.Fori(0, FCH - 1) as i:
                    load(g, use_f(l, f, g, i + 1), first + i * 3 + 2)
                    load(u, use_f(l, f, u, i + 1), first + i * 3 + 3)
                    load(d, use_f(l, f, d, i), first + i * 3 + 4)
                load(g, use_f(l, f, g, FCH), first + (3 * FCH - 1))

            load(0, 0, 0)
            sp.dma_start(x[:], x_in).then_inc(x_landed, 16)
            with sp.Fori(0, DEPTH) as l:
                load_swiglu(l, 0, l * PER_LAYER)
                for j in range(N_MIX):
                    load(slot_mix(j), use_mix(l, j), l * PER_LAYER + (3 * FCH + j))
                    if j == 0:
                        sp.wait_ge(x_ready, l * 12 + 4)
                        for dst, src in ((bd, block_diag), (wt, sgu_wt), (sbias, sgu_bias)):
                            sp.dma_start(dst[:].rearrange("p a c -> p (a c)"),
                                         src[:, ds(l, 1), :].rearrange("p a c -> p (a c)")).then_inc(small_landed, 16)
                load(ROLES[1][0], use_f(l, 1, ROLES[1][0], 0), l * PER_LAYER + (3 * FCH + N_MIX))
                load_swiglu(l, 1, l * PER_LAYER + (3 * FCH + N_MIX))
                load(0, use_f(l + 1, 0, 0, 0), l * PER_LAYER + PER_LAYER)
            for b in range(4):
                sp.wait_ge(out_ready, b + 1)
                sp.dma_start(out[:, 2 * b:2 * b + 2, :], xg[b // 2][:, 2 * (b % 2):2 * (b % 2) + 2, :])\
                    .then_inc(out_landed, 16)
            sp.wait_ge(out_landed, 64)

        @block.tensor
        def _(pe):
            mm = nc.tensor.matmul

            def mm3(dst, wh, wl, mh, ml, start, stop, shared=False):
                mm(dst, wh, mh, start=start, stop=False, skip_group_check=shared)
                mm(dst, wh, ml, start=False, stop=False, skip_group_check=shared)
                return mm(dst, wl, mh, start=False, stop=stop, skip_group_check=shared)

            def cols(slot, dst, m, wait_x=None, between=(None, None)):
                wh = whi[slot][:].rearrange("p (k c) -> p k c", k=KT)
                wl = wlo[slot][:].rearrange("p (k c) -> p k c", k=KT)
                for k in range(KT):
                    if wait_x is not None:
                        pe.wait_ge(xlo_ready, wait_x + (k + 1))
                    last = mm3(dst[:, m, :], wh[:, k, m * P:m * P + P], wl[:, k, m * P:m * P + P],
                               xhi[:, k, :], xlo[:, k, :], k == 0, k == KT - 1)
                    if k == between[0]:
                        between[1]()
                return last

            def toks(slot, dst, t):
                wh = whi[slot][:].rearrange("p (k c) -> p k c", k=KT)
                wl = wlo[slot][:].rearrange("p (k c) -> p k c", k=KT)
                for k in range(KT):
                    last = mm3(dst[:, t, :], xhi[:, k, t * P:t * P + P], xlo[:, k, t * P:t * P + P],
                               wh[:, k, :], wl[:, k, :], k == 0, k == KT - 1)
                return last

            def sum_squares(norm, tiles):
                for k in tiles:
                    for t in range(TT):
                        last = mm(normsum[:, t:t + 1], xsq[:, k, t * P:t * P + P], ones_col[:],
                                  start=(k == 0 and t == 0), stop=(k == tiles[-1]), skip_group_check=True)
                return last

            def spread_rinv(norm):
                pe.wait_ge(rrows_ready, norm + 1)
                for t in range(TT):
                    last = mm(rinv_ps[:, t * P:t * P + P], rinv_rows[:, t, :], ident[:], start=True, stop=True)
                last.then_inc(rps_ready, 1)

            def first_chunk(slot, use, norm, dst):
                pe.wait_ge(lo_ready[slot], use + 2)
                cols(slot, dst, 0, wait_x=norm * KT)
                cols(slot, dst, 1).then_inc(chunk_used[slot], 1)

            def second_chunk(slot, use, norm, dst):
                pe.wait_ge(lo_ready[slot], use + 2)

                def sums():
                    pe.wait_ge(xsq_sum, norm * 4 + 4)
                    sum_squares(norm, (0,)).then_inc(normsum_ready, 1)

                cols(slot, dst, 0, between=(SUM_AT, sums))
                cols(slot, dst, 1, between=(SPREAD_AT, lambda: spread_rinv(norm))).then_inc(chunk_used[slot], 1)

            def accumulate(slot, use, hi_in, lo_in, first, last, between=None):
                pe.wait_ge(lo_ready[slot], use + 2)
                wh = whi[slot][:].rearrange("p (k n) -> p k n", k=2)
                wl = wlo[slot][:].rearrange("p (k n) -> p k n", k=2)

                def one(k, m, stop):
                    return mm3(acc[:, m, :], wh[:, k, m * P:m * P + P], wl[:, k, m * P:m * P + P],
                               hi_in[:, k, :], lo_in[:, k, :], first and k == 0 and m % 2 == 0, stop, shared=True)

                if not last:
                    for k in range(2):
                        for m in range(KT):
                            ins = one(k, m, False)
                        if between is not None and k == 0:
                            between()
                    ins.then_inc(chunk_used[slot], 1)
                else:
                    for b in range(4):
                        for m in (2 * b, 2 * b + 1):
                            for k in range(2):
                                ins = one(k, m, k == 1)
                        ins.then_inc(acc_done, 1)
                    mm(normsum[:, 0:1], ident[:], ones_col[:], start=True, stop=True).then_inc(chunk_used[slot], 1)

            def swiglu(l, f, norm):
                g, u, d = ROLES[f]
                done = l * (2 * FCH) + f * FCH
                first_chunk(g, use_f(l, f, g, 0), norm, zb[0])

                def up_chunk(i):
                    pe.wait_ge(lo_ready[u], use_f(l, f, u, i) + 2)
                    cols(u, zb[1], 0)
                    cols(u, zb[1], 1).then_inc(chunk_used[u], 1)

                def triple(i, first):
                    pe.wait_ge(lo_ready[g], use_f(l, f, g, i) + 2)
                    pe.wait_ge(gsc_ready, done + i)
                    cols(g, zb[0], 0)
                    cols(g, zb[0], 1).then_inc(chunk_used[g], 1)
                    pe.wait_ge(up_ready, done + i)
                    up_chunk(i)
                    pe.wait_ge(alo_ready, done + i)
                    accumulate(d, use_f(l, f, d, i - 1), ahi, alo, first, False)

                second_chunk(u, use_f(l, f, u, 0), norm, zb[1])
                triple(1, True)
                with pe.Fori(2, FCH) as i:
                    triple(i, False)
                pe.wait_ge(alo_ready, done + FCH)
                accumulate(g, use_f(l, f, g, FCH), ahi_last, alo_last, False, True)

            def score(l, j):
                if j == 0:
                    pe.wait_ge(k_ready, l + 1)
                    pe.wait_ge(q_ready, l + 1)
                    left, right = kk, qq
                else:
                    pe.wait_ge(wq_ready, l * 8 + j)
                    pe.wait_ge(wk_ready, l * 8 + j)
                    left = right = wqk[j % 2]
                if j == 1:
                    for h in range(HEADS):
                        last = mm(cross_ps[:, h, :], left[:, h, 0:P], right[:, h, P:2 * P], start=True, stop=True)
                else:
                    if j >= 2:
                        pe.wait_ge(score_kept, l * 8 + max(1, j - 2))
                    for h in range(HEADS):
                        for t in range(TT):
                            queries = right[:, h, t * P:t * P + P]
                            if j == 0:
                                dst = diag_ps[:, h * TT + t, :]
                            else:
                                half = HALVES[j - 2]
                                queries = queries.rearrange("p (n two s) -> p n two s", two=2, s=half)[:, :, 1, :]
                                dst = bank(j % 2)[:, (h * TT + t) * 64:(h * TT + t) * 64 + 64]\
                                    .rearrange("p (n s) -> p n s", s=half)
                            n_left = 64 if j == 2 else P
                            last = mm(dst[0:n_left], left[:, h, t * P:t * P + n_left], queries, start=True, stop=True)
                last.then_inc(score_done, 1)

            def lru_gates(l):
                pe.wait_ge(small_landed, l * 48 + 48)
                pe.wait_ge(xc_ready, l * 2 + 2)
                for a in range(2):
                    for m in range(2):
                        last = mm(gate_ps[:, a, m, :], bd[:, 2 * a + m, :], xc[:, m, :], start=True, stop=True)
                last.then_inc(gates_done, 1)

            def sgu_mix(l):
                pe.wait_ge(v_ready, l + 1)
                pe.wait_ge(wt_masked, l + 1)
                pe.wait_ge(cross_kept, l + 1)
                pe.wait_ge(group_landed, 16)
                for j in range(2):
                    mm(z_ps[:, j, :], group_of[:, j, :], sbias[:].rearrange("g t s -> g (t s)"),
                       start=(j == 0), stop=False, skip_group_check=True)
                for grp in range(4):
                    lo_p = 64 * (grp % 2)
                    for t in range(TT):
                        last = mm(z_ps[lo_p:lo_p + 64, grp // 2, t * P:t * P + P], v_z[:, t, 64 * grp:64 * grp + 64],
                                  wt[:, grp, :], start=False, stop=True, skip_group_check=True)
                last.then_inc(z_done, 1)

            def sums_bc(l, c):
                pe.wait_ge(ysq_ready, l * 2 + c + 1)
                for t in range(TT):
                    for j in range(2):
                        last = mm(sumsq_bc[:, c, t, j, :], ysq[c][:, j, t * P:t * P + P], half_ones[:],
                                  start=True, stop=True)
                last.then_inc(sumbc_done, 1)

            def spread_bc(l, c):
                pe.wait_ge(rows_bc_ready, l * 2 + c + 1)
                if c == 0:
                    pe.wait_ge(rg_tanh, l * 4 + 4)
                else:
                    pe.wait_ge(yc_ready, l + 1)
                for j in range(2):
                    for t in range(TT):
                        last = mm(spread_bc_ps[c][:, j, t * P:t * P + P], rows_bc[:, c, t, j, :], ident[:],
                                  start=True, stop=True)
                last.then_inc(spread_bc_done, 1)

            def outputs_a(l):
                pe.wait_ge(vals_ready, l * 4 + 4)
                pe.wait_ge(z_free[0], l * 6 + 6)
                pe.wait_ge(z_free[1], l * 6 + 6)
                pe.wait_ge(score_kept, l * 8 + 8)
                for h in range(HEADS):
                    v0, v1 = vals[:, 0, h * P:h * P + P], vals[:, 1, h * P:h * P + P]
                    mm(o_ps[:, h, 0:P], v0, scores[:, h * TT, :], start=True, stop=True)
                    mm(o_ps[:, h, P:2 * P], v0, cross[:, h, :], start=True, stop=False)
                    last = mm(o_ps[:, h, P:2 * P], v1, scores[:, h * TT + 1, :], start=False, stop=True)
                last.then_inc(o_done, 1)

            def sums_a(l):
                pe.wait_ge(osq_ready, l + 1)
                for t in range(TT):
                    for h in range(HEADS):
                        last = mm(sumsq_a[:, t, h:h + 1], osq[:, h, t * P:t * P + P], ones_col[:],
                                  start=True, stop=True)
                last.then_inc(suma_done, 1)

            def spread_a(l):
                pe.wait_ge(rows_a_ready, l + 1)
                pe.wait_ge(og_ready, l + 1)
                for h in range(HEADS):
                    for t in range(TT):
                        last = mm(spread_a_ps[:, h, t * P:t * P + P], rows_a[:, t, h, :], ident[:],
                                  start=True, stop=True)
                    if h % 2 == 1:
                        last.then_inc(spread_a_done, 1)

            def mixer(l, norm):
                for n in range(N_IN):
                    slot, dst = slot_mix(n), zb[n % 2]
                    if n == 0:
                        first_chunk(slot, use_mix(l, n), norm, dst)
                    elif n == 1:
                        second_chunk(slot, use_mix(l, n), norm, dst)
                    else:
                        pe.wait_ge(lo_ready[slot], use_mix(l, n) + 2)
                        if n >= 2:
                            pe.wait_ge(z_free[n % 2], l * 6 + n // 2)
                        part = toks if n in (6, 7, 8) else cols
                        part(slot, dst, 0)
                        part(slot, dst, 1).then_inc(chunk_used[slot], 1)
                    if n == 5:
                        score(l, 0)
                    if n >= 5:
                        score(l, n - 4)
                    if n == 7:
                        lru_gates(l)

                def out(c, tile, first, last, between=None):
                    j = N_IN + c
                    accumulate(slot_mix(j), use_mix(l, j), yhi[:, tile:tile + 2, :], ylo[:, tile:tile + 2, :],
                               first, last, between)

                sums_bc(l, 0)
                score(l, 8)
                spread_bc(l, 0)
                sgu_mix(l)
                outputs_a(l)
                sums_bc(l, 1)

                def small():
                    spread_bc(l, 1)
                    sums_a(l)

                pe.wait_ge(ylbc, l * 2 + 1)
                out(0, 4, True, False, small)
                spread_a(l)
                pe.wait_ge(ylbc, l * 2 + 2)
                out(1, 6, False, False)
                pe.wait_ge(yla, l * 2 + 1)
                out(2, 0, False, False)
                pe.wait_ge(yla, l * 2 + 2)
                out(3, 2, False, True)

            for slot in range(3):
                pe.sem_inc(chunk_used[slot], 1)
            pe.wait_ge(ones_made, 3)
            pe.wait_ge(ident_landed, 16)
            with pe.Fori(0, DEPTH) as l:
                swiglu(l, 0, l * 3)
                mixer(l, l * 3 + 1)
                swiglu(l, 1, l * 3 + 2)
            pe.wait_ge(xsq_sum, 3 * DEPTH * 4 + 2)
            sum_squares(3 * DEPTH, (0, 1))
            pe.wait_ge(xsq_act, 3 * DEPTH * 2 + 2)
            sum_squares(3 * DEPTH, (6, 7)).then_inc(normsum_ready, 1)
            spread_rinv(3 * DEPTH)

        @block.scalar
        def _(act):
            A = nc.scalar.activation
            act.dma_start(par_all[:], params).then_inc(par_landed, 16)
            act.dma_start(ident[:], identity).then_inc(ident_landed, 16)
            act.dma_start(group_of[:].rearrange("g j p -> g (j p)"), group_rows).then_inc(group_landed, 16)
            nc.scalar.preload_act_table(ACT.Silu)
            for dst, src in ((bc[:].rearrange("p h t -> p (h t)")[:, 0:N_MASK], masks), (tri[:], causal)):
                act.dma_start(dst, src).then_inc(const_landed, 16)

            def hi(slot, use):
                act.wait_ge(landed[slot], use * 16 + 16)
                act.wait_ge(chunk_used[slot], use + 1)
                nc.scalar.copy(whi[slot][:], raw[slot][:]).then_inc(hi_ready[slot], 1)

            def hi_mix(l, j):
                hi(slot_mix(j), use_mix(l, j))

            def split_x(col, m):
                A(xhi[:, m, :], x[:, m, :], ACT.Copy, scale=par[:, col + m:col + m + 1]).then_inc(xhi_ready, 1)

            def square_x(norm, b):
                nc.scalar.square(xsq[:, 2 * b:2 * b + 2, :], x[:, 2 * b:2 * b + 2, :]).then_inc(xsq_act, 1)

            def splits(norm, col):
                for b in range(4):
                    act.wait_ge(x_ready, norm * 4 + (b + 1))
                    split_x(col, 2 * b)
                    split_x(col, 2 * b + 1)
                    if b == 2:
                        square_x(norm, 2)

            def norm_stats(norm, last=False):
                act.wait_ge(normsum_ready, norm + 1)
                A(tokvar[:], normsum, ACT.Identity, bias=eps_col[:], scale=1.0 / D).then_inc(var_ready, 1)
                act.wait_ge(rtok_ready, norm + 1)
                A(rinv_rows[:], rinv_tok[:].unsqueeze(2).to_broadcast([P, TT, P]), ACT.Copy).then_inc(rrows_ready, 1)
                if not last:
                    act.wait_ge(rps_ready, norm + 1)
                    nc.scalar.copy(rinv[:], rinv_ps).then_inc(rinv_ready, 1)

            def swiglu(l, f, norm):
                g, u, d = ROLES[f]
                done = l * (2 * FCH) + f * FCH

                def silu(i):
                    act.wait_ge(gsc_ready, done + i + 1)
                    A(gact[:], gsc[:], ACT.Silu).then_inc(gact_ready, 1)

                def round_act(i):
                    act.wait_ge(actf_ready, done + i + 1)
                    act.wait_ge(chunk_used[d], use_f(l, f, d, i) + 1)
                    nc.scalar.copy(ahi[:], act_f[:]).then_inc(ahi_ready, 1)

                def triple(i):
                    silu(i)
                    hi(u, use_f(l, f, u, i + 1))
                    round_act(i)
                    hi(d, use_f(l, f, d, i))

                nc.scalar.preload_act_table(ACT.Silu)
                hi(g, use_f(l, f, g, 1))
                norm_stats(norm)
                triple(0)
                with act.Fori(1, FCH - 1) as i:
                    hi(g, use_f(l, f, g, i + 1))
                    triple(i)
                hi(g, use_f(l, f, g, FCH))
                silu(FCH - 1)
                hi(u, use_f(l, f, u, FCH))
                act.wait_ge(actf_ready, done + FCH)
                nc.scalar.copy(ahi_last, act_f[:]).then_inc(ahi_ready, 1)
                if f == 0:
                    vectors(l)

            def vectors(l):
                lam, tmp = par[:, C_LAM:C_LAM + 2], vec[:, 0:2]
                A(tmp, lam, ACT.Abs).then_inc(vec_act, 1)
                A(vec[:, 2:4], lam, ACT.Relu, scale=-1.0).then_inc(vec_act, 1)
                act.wait_ge(vec_act, l * 5 + 1)
                A(tmp, tmp, ACT.Exp, scale=-1.0).then_inc(vec_act, 1)
                act.wait_ge(vec_dve, l * VEC_STEPS + 2)
                A(vec[:, 8:16], vec[:, 8:16], ACT.Exp).then_inc(vec_act, 1)
                act.wait_ge(vec_act, l * 5 + 3)
                A(tmp, tmp, ACT.Ln, bias=1.0).then_inc(vec_act, 1)

            def mixer(l):
                def exp_level(j):
                    act.wait_ge(dist_ready, l * 8 + j)
                    A(dist[j % 2][:], dist[j % 2][:], ACT.Exp).then_inc(exp_ready, 1)

                def vals_out(n):
                    act.wait_ge(chunk_used[slot_mix(n)], use_mix(l, n) + 2)
                    c = (n - 6) * CW
                    A(vals[:, 0, c:c + CW], zb[n % 2][:, 0, :], ACT.Copy, scale=rinv_tok[:, 0:1]).then_inc(vals_ready, 1)
                    A(vals[:, 1, c:c + CW], zb[n % 2][:, 1, :], ACT.Copy, scale=rinv_tok[:, 1:2])\
                        .then_inc(vals_ready, 1)
                    act.wait_ge(vals_ready, l * 4 + (2 * (n - 6) + 2))
                    act.sem_inc(z_free[n % 2], 1)

                for n in range(10):
                    hi_mix(l, n + 3)
                    if n == 0:
                        norm_stats(l * 3 + 1)
                    if n in (0, 1):
                        act.wait_ge(f_evac, l * 2 + n + 1)
                        A(fz[:, 2 * n:2 * n + 2, :], fz[:, 2 * n:2 * n + 2, :], ACT.Sigmoid).then_inc(f_sig, 1)
                    if n == 2:
                        act.wait_ge(clamp_ready, l + 1)
                        A(fz[:], fz[:], ACT.Ln).then_inc(logf_ready, 1)
                    if n == 3:
                        act.wait_ge(q_evac, l * 2 + 2)
                        A(qs[:], qz[:], ACT.Sigmoid).then_inc(q_sig, 1)
                        exp_level(1)
                    if n == 4:
                        exp_level(2)
                    if n == 6:
                        vals_out(n)
                        nc.scalar.copy(cross[:].rearrange("p a t -> p (a t)"), bank(7)).then_inc(cross_kept, 1)
                    if n == 7:
                        act.wait_ge(vec_dve, (l + 1) * VEC_STEPS)
                        act.wait_ge(gates_done, l + 1)
                        for m in range(2):
                            A(rt[:, m, :], gate_ps[:, 0, m, :], ACT.Tanh, bias=par[:, C_HBA + m:C_HBA + m + 1],
                              scale=0.5).then_inc(rg_tanh, 1)
                            A(gt[:, m, :], gate_ps[:, 1, m, :], ACT.Tanh, bias=par[:, C_HBX + m:C_HBX + m + 1],
                              scale=0.5).then_inc(rg_tanh, 1)
                        vals_out(n)
                    if n == 8:
                        act.wait_ge(chunk_used[slot_mix(n)], use_mix(l, n) + 2)
                        for t in range(TT):
                            A(v_z[:, t, :], zb[n % 2][:, t, :], ACT.Copy, scale=rinv_tok[:, t:t + 1])\
                                .then_inc(v_evac, 1)
                        act.wait_ge(v_evac, l * 2 + 2)
                        act.sem_inc(z_free[n % 2], 1)
                    if 5 <= n:
                        exp_level(n - 2)
                    if n == 8:
                        for m in range(2):
                            c4 = par[:, C_C4 + m:C_C4 + m + 1]
                            A(dec[:, m, :], rt[:, m, :], ACT.Exp, bias=c4, scale=c4).then_inc(dec_ready, 1)
                        for m in range(2):
                            c4 = par[:, C_C4 + m:C_C4 + m + 1]
                            A(th[:, m, :], rt[:, m, :], ACT.Tanh, bias=c4, scale=c4).then_inc(th_ready, 1)
                exp_level(8)
                act.wait_ge(v_evac, l * 2 + 2)
                A(v_z[:], v_z[:], ACT.Gelu_apprx_tanh).then_inc(v_gelu, 1)
                act.wait_ge(gate_evac, l + 1)
                A(gate_z, gate_z, ACT.Gelu_apprx_tanh).then_inc(gate_gelu, 1)
                act.wait_ge(u_evac, l + 1)
                A(u_z, u_z, ACT.Gelu_apprx_tanh).then_inc(u_gelu, 1)
                act.wait_ge(mult2_ready, l + 1)
                A(rt[:], th[:], ACT.Sqrt, scale=-0.25).then_inc(mult_ready, 1)
                act.wait_ge(v_cent, l + 1)
                act.wait_ge(mult_ready, l + 1)
                nc.scalar.square(v_squares[:], v_z[:]).then_inc(v_sq, 1)
                hi_mix(l, 13)

                def squares_bc(c):
                    nc.scalar.square(ysq[c][:], y_bc[:, 2 * c:2 * c + 2, :]).then_inc(ysq_ready, 1)

                def rms_of_bc(c):
                    act.wait_ge(sumbc_done, l * 2 + c + 1)
                    A(inv_bc[:, c], sumsq_bc[:, c], ACT.Sqrt, bias=eps_col[:], scale=1.0 / 64).then_inc(rms_bc, 1)
                    act.wait_ge(inv_bc_ready, l * 2 + c + 1)
                    A(rows_bc[:, c].rearrange("p t j (g s) -> p (t j g) s", s=64),
                      inv_bc[:, c].rearrange("p t j g -> p (t j g)").unsqueeze(2).to_broadcast([P, 8, 64]),
                      ACT.Copy).then_inc(rows_bc_ready, 1)

                def round_bc(c):
                    act.wait_ge(nbc_ready, l * 4 + 2 * c + 2)
                    nc.scalar.copy(yhi[:, 4 + 2 * c:6 + 2 * c, :], y_bc[:, 2 * c:2 * c + 2, :]).then_inc(yhbc, 1)

                act.wait_ge(yb_ready, l + 1)
                squares_bc(0)
                rms_of_bc(0)
                act.wait_ge(g_evac, l * 2 + 2)
                A(qs[:], gz[:], ACT.Sigmoid).then_inc(g_sig, 1)
                round_bc(0)
                act.wait_ge(yc_ready, l + 1)
                squares_bc(1)
                act.wait_ge(o_done, l + 1)
                nc.scalar.square(osq[:], o_ps).then_inc(osq_ready, 1)
                rms_of_bc(1)
                hi_mix(l, 14)
                round_bc(1)
                act.wait_ge(suma_done, l + 1)
                A(inv_a[:], sumsq_a, ACT.Sqrt, bias=eps_col[:], scale=1.0 / 128).then_inc(rms_a, 1)
                act.wait_ge(inv_a_ready, l + 1)
                A(rows_a.rearrange("p t h s -> p (t h) s"),
                  inv_a[:].rearrange("p t h -> p (t h)").unsqueeze(2).to_broadcast([P, TT * HEADS, P]), ACT.Copy)\
                    .then_inc(rows_a_ready, 1)
                for p in range(2):
                    act.wait_ge(na_ready, l * 2 + p + 1)
                    nc.scalar.copy(yhi[:, 2 * p:2 * p + 2, :], gz[:, 2 * p:2 * p + 2, :]).then_inc(yha, 1)
                hi_mix(l, 15)
                hi(ROLES[1][0], use_f(l, 1, ROLES[1][0], 0))

            hi(0, 0)
            act.wait_ge(par_ready, 1)
            act.wait_ge(ones_made, 1)
            splits(0, C_N1)
            with act.Fori(0, DEPTH) as l:
                hi(1, use_f(l, 0, 1, 0))
                square_x(l * 3, 3)
                swiglu(l, 0, l * 3)
                hi_mix(l, 1)
                splits(l * 3 + 1, C_NM)
                square_x(l * 3 + 1, 3)
                hi_mix(l, 2)
                mixer(l)
                hi(ROLES[1][1], use_f(l, 1, ROLES[1][1], 0))
                splits(l * 3 + 2, C_N2)
                square_x(l * 3 + 2, 3)
                swiglu(l, 1, l * 3 + 2)
                act.wait_ge(par_ready, l + 2)
                splits(l * 3 + 3, C_N1)
            square_x(3 * DEPTH, 3)
            norm_stats(3 * DEPTH, last=True)

        @block.gpsimd
        def _(pool):
            G = nc.gpsimd

            pair = [xsq[:, 2 * b:2 * b + 2, :] for b in range(4)]

            def add_pair(norm, b):
                if b > 1:
                    pool.wait_ge(xsq_act, norm * 2 + (b - 1))
                    pool.wait_ge(xsq_sum, norm * 4 + (b - 1))
                G.tensor_tensor(pair[0], pair[0], pair[b], ALU.add).then_inc(xsq_sum, 1)

            def squares(norm):
                for b in range(2):
                    pool.wait_ge(x_ready, norm * 4 + (b + 1))
                    G.tensor_tensor(pair[b], x[:, 2 * b:2 * b + 2, :], x[:, 2 * b:2 * b + 2, :], ALU.mult)\
                        .then_inc(xsq_pool, 1)
                pool.wait_ge(xsq_pool, norm * 2 + 2)
                add_pair(norm, 1)
                add_pair(norm, 2)

            def add_last(norm):
                add_pair(norm, 3)
                pool.wait_ge(xsq_sum, norm * 4 + 3)
                G.tensor_tensor(xsq[:, 0, :], xsq[:, 0, :], xsq[:, 1, :], ALU.add).then_inc(xsq_sum, 1)

            def rsqrt(norm):
                pool.wait_ge(var_ready, norm + 1)
                G.tensor_tensor(rinv_tok[:], tokvar[:], neg_half[:, 0:TT], ALU.pow).then_inc(rtok_ready, 1)

            def distances(l, j):
                if j > 2:
                    pool.wait_ge(wq_ready, l * 8 + (j - 2))
                    pool.wait_ge(wk_ready, l * 8 + (j - 2))
                h = (128,) + HALVES
                h = h[j - 1]
                buf = dist[j % 2]
                if h == 128:
                    b = bc[:].rearrange("p h (c s) -> p h c s", s=SUB)
                    o = buf[:].rearrange("p h (c s) -> p h c s", s=SUB)

                    def end(c):
                        return b[:, :, c, SUB - 1:SUB].to_broadcast([P, HEADS, SUB])
                    G.tensor_tensor(o[:, :, 0, :], end(0), b[:, :, 0, :], ALU.subtract).then_inc(dist_part, 1)
                    G.tensor_tensor(o[:, :, 1, :], end(1), b[:, :, 1, :], ALU.subtract)
                    G.tensor_copy(o[:, :, 2, :], b[:, :, 2, :])
                    pool.wait_ge(dist_part, l + 1)
                    G.tensor_tensor(o[:, :, 0, :], o[:, :, 0, :], end(1), ALU.add)
                    G.tensor_tensor(o[:, :, 3, :], b[:, :, 3, :], end(2), ALU.add).then_inc(dist_ready, 1)
                    return
                b = bc[:].rearrange("p h (n two s) -> p (h n) two s", two=2, s=h)
                o = buf[:].rearrange("p h (n two s) -> p (h n) two s", two=2, s=h)
                end = b[:, :, 0, h - 1:h].to_broadcast([P, HEADS * SEQ // (2 * h), h])
                G.tensor_tensor(o[:, :, 0, :], end, b[:, :, 0, :], ALU.subtract)
                if h == SUB:
                    G.tensor_copy(o[:, :, 1, :], b[:, :, 1, :]).then_inc(dist_ready, 1)
                else:
                    G.tensor_tensor(o[:, :, 1, :], b[:, :, 1, :], end, ALU.subtract).then_inc(dist_ready, 1)

            def weigh_keys(l, j):
                h = ((128,) + HALVES)[j - 1]
                pool.wait_ge(exp_ready, l * 8 + j)
                if j > 2:
                    pool.wait_ge(score_done, l * 9 + (j - 1))
                sel = "p h (n two s) -> p (h n) two s"
                o, e, k = (t[:].rearrange(sel, two=2, s=h)[:, :, 0, :] for t in (wqk[j % 2], dist[j % 2], kk))
                G.tensor_tensor(o, e, k, ALU.mult).then_inc(wk_ready, 1)

            def mixer(l):
                pool.wait_ge(b_ready, l + 1)
                distances(l, 1)
                distances(l, 2)
                mean = v_stat[:, 0:8].unsqueeze(2).to_broadcast([P, 8, 64])
                vg = v_z[:].rearrange("p t (g c) -> p (t g) c", c=64)
                for j in range(1, 9):
                    if j == 8:
                        pool.wait_ge(v_mean, l + 1)
                        G.tensor_tensor(vg, vg, mean, ALU.subtract).then_inc(v_cent, 1)
                    weigh_keys(l, j)
                    if j == 6:
                        pool.wait_ge(dec_ready, l * 2 + 2)
                        G.tensor_tensor(dec_sq, dec[:], dec[:], ALU.mult).then_inc(dec2_ready, 1)
                    if j + 2 <= 8:
                        distances(l, j + 2)
                pool.wait_ge(mult_ready, l + 1)
                pool.wait_ge(lin_part, l + 1)
                G.tensor_tensor(lin[:], lin[:], rt[:], ALU.mult).then_inc(lin_ready, 1)
                pool.wait_ge(v_var, l + 1)
                G.tensor_tensor(v_stat[:, 16:24], v_stat[:, 8:16], neg_half[:], ALU.pow).then_inc(v_rstd, 1)
                pool.wait_ge(v_rstd, l + 1)
                pool.wait_ge(v_sq, l + 1)
                rstd = v_stat[:, 16:24].unsqueeze(2).to_broadcast([P, 8, 64])
                G.tensor_tensor(vg, vg, rstd, ALU.mult).then_inc(v_ready, 1)
                pool.wait_ge(g_sig, l + 1)
                G.tensor_tensor(gz[:], qs[:], gz[:], ALU.mult).then_inc(gs_ready, 1)

            G.memset(reset[:], 1.0).then_inc(setup_pool, 1)
            G.memset(neg_half[:], -0.5).then_inc(setup_pool, 1)
            pool.wait_ge(setup_pool, 2)
            G.memset(reset[:].rearrange("p (n s) -> p n s", s=SUB)[:, :, 0:1], 0.0)
            G.memset(scores[:], 0.0).then_inc(setup_pool, 1)
            pool.wait_ge(x_landed, 16)
            pool.sem_inc(x_ready, 4)
            squares(0)
            pool.wait_ge(const_landed, 16 * N_CONST)
            G.tensor_copy(mask[:], bc[:].rearrange("p h t -> p (h t)")[:, 0:N_MASK])\
                .then_inc(setup_pool, 1)
            with pool.Fori(0, DEPTH) as l:
                add_last(l * 3)
                rsqrt(l * 3)
                squares(l * 3 + 1)
                add_last(l * 3 + 1)
                rsqrt(l * 3 + 1)
                mixer(l)
                squares(l * 3 + 2)
                add_last(l * 3 + 2)
                rsqrt(l * 3 + 2)
                squares(l * 3 + 3)
            rsqrt(3 * DEPTH)

        @block.vector
        def _(dve):
            V = nc.vector

            def lo(slot, use):
                dve.wait_ge(hi_ready[slot], use + 1)
                V.tensor_tensor(wlo[slot][:], raw[slot][:], whi[slot][:].bitcast(F32), ALU.subtract)\
                    .then_inc(lo_ready[slot], 1)

            def lo_mix(l, j):
                lo(slot_mix(j), use_mix(l, j))

            def split_x(norm, col, m):
                dve.wait_ge(xhi_ready, norm * KT + m + 1)
                V.scalar_tensor_tensor(xlo[:, m, :], x[:, m, :], par[:, col + m:col + m + 1],
                                       xhi[:, m, :].bitcast(F32), ALU.mult, ALU.subtract).then_inc(xlo_ready, 1)

            def residual(update, b, factor):
                dve.wait_ge(acc_done, update * 4 + b + 1)
                V.scalar_tensor_tensor(x[:, 2 * b:2 * b + 2, :], acc[:, 2 * b:2 * b + 2, :], factor,
                                       x[:, 2 * b:2 * b + 2, :], ALU.mult, ALU.add).then_inc(x_ready, 1)

            def residual_and_split(update, norm, col, factor):
                residual(update, 0, factor)
                for b in range(1, 4):
                    residual(update, b, factor)
                    split_x(norm, col, 2 * b - 2)
                    split_x(norm, col, 2 * b - 1)
                split_x(norm, col, 6)
                split_x(norm, col, 7)

            logits = par_all[:, 0:DEPTH, C_LBL:C_LBL + 4]
            top = vec[:, 4:8]
            vec_e = vec[:, 8:16].rearrange("p (l c) -> p l c", l=DEPTH)
            vec_b = vec[:, 16:24].rearrange("p (l c) -> p l c", l=DEPTH)

            def vec_step(l, n, ins):
                ins.then_inc(vec_dve, 1)
                dve.wait_ge(vec_dve, l * VEC_STEPS + n)

            def vectors_before(l):
                vec_step(l, 1, V.tensor_tensor(top, logits[:, 0, :], logits[:, 1, :], ALU.max))
                V.tensor_tensor(vec_e, logits, top.unsqueeze(1).to_broadcast([P, DEPTH, 4]), ALU.subtract)\
                    .then_inc(vec_dve, 1)
                V.tensor_scalar(par[:, C_HBA:C_HBA + 4], par[:, C_BA:C_BA + 4], 0.5, None, ALU.mult)

            def vectors_after(l):
                dve.wait_ge(vec_act, l * 5 + 4)
                vec_step(l, 3, V.tensor_tensor(top, vec_e[:, 0, :], vec_e[:, 1, :], ALU.add))
                vec_step(l, 4, V.reciprocal(top, top))
                vec_step(l, 5, V.tensor_tensor(vec_e, vec_e, top.unsqueeze(1).to_broadcast([P, DEPTH, 4]), ALU.mult))
                V.tensor_tensor(vec_b[:, 0, :], vec_e[:, 0, :], vec_e[:, 0, :], ALU.subtract)
                vec_step(l, 6, V.tensor_tensor(top, vec_e[:, 0, :], vec_e[:, 1, :], ALU.add))
                vec_step(l, 7, V.tensor_tensor(vec_b[:, 1, :], top, vec_e[:, 0, :], ALU.subtract))
                vec_step(l, 8, V.tensor_copy(par[:, C_LB:C_LB + 4],
                                             vec_b[:, ds(l, 1), :].rearrange("p a c -> p (a c)")))
                V.tensor_scalar(par[:, C_OML:C_OML + 4], par[:, C_LB:C_LB + 4], -1.0, 1.0, ALU.mult, ALU.add)
                dve.wait_ge(vec_act, l * 5 + 5)
                c4 = par[:, C_C4:C_C4 + 2]
                vec_step(l, 9, V.tensor_tensor(c4, vec[:, 0:2], vec[:, 2:4], ALU.add))
                V.tensor_scalar(c4, c4, -4.0, None, ALU.mult).then_inc(vec_dve, 1)

            rinv2 = rinv[:].unsqueeze(1).to_broadcast([P, 2, SEQ])

            def swiglu(l, f, norm):
                g, u, d = ROLES[f]
                done = l * (2 * FCH) + f * FCH

                def gate(i):
                    dve.wait_ge(rinv_ready, norm + 1)
                    dve.wait_ge(chunk_used[g], use_f(l, f, g, i) + 2)
                    V.tensor_tensor(gsc[:], zb[0], rinv2, ALU.mult).then_inc(gsc_ready, 1)

                def gated(i):
                    dve.wait_ge(chunk_used[u], use_f(l, f, u, i) + 2)
                    dve.wait_ge(gact_ready, done + i + 1)
                    V.tensor_tensor(up[:], zb[1], gact[:], ALU.mult).then_inc(up_ready, 1)
                    dve.wait_ge(up_ready, done + i + 1)
                    V.tensor_tensor(act_f[:], up[:], rinv2, ALU.mult).then_inc(actf_ready, 1)

                def split_act(i):
                    dve.wait_ge(ahi_ready, done + i + 1)
                    V.tensor_tensor(alo[:], act_f[:], ahi[:].bitcast(F32), ALU.subtract).then_inc(alo_ready, 1)

                def rest(i):
                    gated(i)
                    lo(u, use_f(l, f, u, i + 1))
                    split_act(i)
                    lo(d, use_f(l, f, d, i))

                if f == 0:
                    vectors_before(l)
                lo(g, use_f(l, f, g, 1))
                gate(0)
                rest(0)
                with dve.Fori(1, FCH - 1) as i:
                    gate(i)
                    lo(g, use_f(l, f, g, i + 1))
                    rest(i)
                gate(FCH - 1)
                lo(g, use_f(l, f, g, FCH))
                gated(FCH - 1)
                dve.wait_ge(ahi_ready, done + FCH)
                V.tensor_tensor(alo_last, act_f[:], ahi_last.bitcast(F32), ALU.subtract).then_inc(alo_ready, 1)
                lo(u, use_f(l, f, u, FCH))
                if f == 0:
                    vectors_after(l)

            def mixer(l, norm):
                def evac(n, dst, signal):
                    dve.wait_ge(rinv_ready, norm + 1)
                    dve.wait_ge(chunk_used[slot_mix(n)], use_mix(l, n) + 2)
                    V.tensor_tensor(dst, zb[n % 2], rinv2, ALU.mult).then_inc(signal, 1)

                def freed(n, signal, value):
                    dve.wait_ge(signal, value)
                    dve.sem_inc(z_free[n % 2], 1)

                def weigh_queries(j):
                    h = ((128,) + HALVES)[j - 1]
                    dve.wait_ge(exp_ready, l * 8 + j)
                    dve.wait_ge(q_ready, l + 1)
                    if j > 2:
                        dve.wait_ge(score_done, l * 9 + (j - 1))
                    sel = "p h (n two s) -> p (h n) two s"
                    o, e, q = (t[:].rearrange(sel, two=2, s=h)[:, :, 1, :] for t in (wqk[j % 2], dist[j % 2], qq))
                    V.tensor_tensor(o, e, q, ALU.mult).then_inc(wq_ready, 1)

                def keep(j):
                    kept = 0 if j == 0 else j - 1
                    dve.wait_ge(score_done, l * 9 + j + 1)
                    dve.sem_inc(keep_begun, 1)
                    if j == 0:
                        V.copy_predicated(scores[:], mask[:, N_MASK - P:].unsqueeze(1).to_broadcast([P, HEADS * TT, P]),
                                          diag_ps).then_inc(score_kept, 1)
                    else:
                        half, n_left = HALVES[j - 2], 64 if j == 2 else P
                        m = mask[0:n_left, (j - 2) * 64:(j - 1) * 64].rearrange("p (n s) -> p n s", s=half)
                        V.copy_predicated(
                            scores[0:n_left].rearrange("p a (n two s) -> p a n two s", two=2, s=half)[:, :, :, 1, :],
                            m.unsqueeze(1).to_broadcast([n_left, HEADS * TT, 64 // half, half]),
                            bank(j % 2)[0:n_left].rearrange("p (a n s) -> p a n s", a=HEADS * TT, s=half))\
                            .then_inc(score_kept, 1)
                    dve.wait_ge(score_kept, l * 8 + kept + 1)

                def conv():
                    for m in range(2):
                        V.tensor_scalar(xc[:, m, :], xpad[:, m, 0:SEQ], par[:, C_CW + m:C_CW + m + 1],
                                        par[:, C_CB + m:C_CB + m + 1], ALU.mult, ALU.add).then_inc(conv_step, 1)
                    for tap in range(1, 4):
                        dve.wait_ge(conv_step, l * 6 + 2 * tap)
                        for m in range(2):
                            c = C_CW + 2 * tap + m
                            V.scalar_tensor_tensor(xc[:, m, :], xpad[:, m, tap:tap + SEQ], par[:, c:c + 1],
                                                   xc[:, m, :], ALU.mult, ALU.add)\
                                .then_inc(conv_step if tap < 3 else xc_ready, 1)

                vg = v_z[:].rearrange("p t (g c) -> p (t g) c", c=64)

                def step(n):
                    if n in (0, 1):
                        evac(n, fz[:, 2 * n:2 * n + 2, :], f_evac)
                        freed(n, f_evac, l * 2 + n + 1)
                    if n in (2, 3):
                        evac(n, qz[:, 2 * n - 4:2 * n - 2, :], q_evac)
                        freed(n, q_evac, l * 2 + (n - 1))
                    if n == 4:
                        evac(n, xpad[:, :, 3:3 + SEQ], xb_evac)
                        freed(n, xb_evac, l + 1)
                    if n == 5:
                        evac(n, gate_z, gate_evac)
                        freed(n, gate_evac, l + 1)
                    if n == 9:
                        evac(n, u_z, u_evac)
                        freed(n, u_evac, l + 1)
                    if n in (10, 11):
                        evac(n, gz[:, 2 * n - 20:2 * n - 18, :], g_evac)
                        freed(n, g_evac, l * 2 + (n - 9))
                    if n == 11:
                        return
                    if 5 <= n <= 9:
                        weigh_queries(n - 3)
                    if n == 10:
                        return
                    lo_mix(l, n + 3)
                    if n == 1:
                        dve.wait_ge(f_sig, l * 2 + 2)
                        for h in range(HEADS):
                            V.tensor_scalar(fz[:, h, :], fz[:, h, :], par[:, C_OML + h:C_OML + h + 1],
                                            par[:, C_LB + h:C_LB + h + 1], ALU.mult, ALU.add).then_inc(forget_ready, 1)
                        dve.wait_ge(forget_ready, l * 4 + 4)
                        V.tensor_scalar(kk[:], fz[:], -1.0, 1.0, ALU.mult, ALU.add).then_inc(k_ready, 1)
                        dve.wait_ge(k_ready, l + 1)
                        V.tensor_scalar(fz[:], fz[:], 2.0 ** -63, None, ALU.max).then_inc(clamp_ready, 1)
                    if n == 2:
                        dve.wait_ge(logf_ready, l + 1)
                        V.tensor_tensor_scan(bc[:].rearrange("p h t -> p (h t)"), reset[:],
                                             fz[:].rearrange("p h t -> p (h t)"), 0.0, ALU.mult, ALU.add)\
                            .then_inc(b_ready, 1)
                    if n == 3:
                        dve.wait_ge(q_sig, l + 1)
                        V.tensor_tensor(qq[:], qz[:], qs[:], ALU.mult).then_inc(q_ready, 1)
                    if n == 4:
                        weigh_queries(1)
                    if 6 <= n <= 9:
                        keep(n - 4)
                    if n == 5:
                        keep(0)
                        conv()
                    if n == 8:
                        dve.wait_ge(rg_tanh, l * 4 + 4)
                        V.scalar_tensor_tensor(lin[:], gt[:], 1.0, xc[:], ALU.add, ALU.mult).then_inc(lin_part, 1)
                    if n == 9:
                        dve.wait_ge(dec2_ready, l + 1)
                        dve.wait_ge(th_ready, l * 2 + 2)
                        V.scalar_tensor_tensor(th[:], dec_sq, 1.0, th[:], ALU.add, ALU.mult)\
                            .then_inc(mult2_ready, 1)

                lo_mix(l, 2)
                dve.wait_ge(setup_pool, 4)
                dve.wait_ge(small_landed, l * 48 + 48)
                V.tensor_tensor(wt[:], wt[:], tri[:].unsqueeze(1).to_broadcast([P, 4, P]), ALU.mult)\
                    .then_inc(wt_masked, 1)
                for n in range(10):
                    step(n)
                weigh_queries(7)
                dve.wait_ge(v_gelu, l + 1)
                V.reduce_sum(v_stat[:, 0:8], vg, AX.X).then_inc(v_part, 1)
                dve.wait_ge(v_part, l * 2 + 1)
                V.tensor_scalar(v_stat[:, 0:8], v_stat[:, 0:8], 1.0 / 64, None, ALU.mult).then_inc(v_mean, 1)
                step(10)
                dve.wait_ge(v_sq, l + 1)
                V.reduce_sum(v_stat[:, 8:16], v_squares[:].rearrange("p j (g c) -> p (j g) c", c=64), AX.X)\
                    .then_inc(v_part, 1)
                dve.wait_ge(v_part, l * 2 + 2)
                V.tensor_scalar(v_stat[:, 8:16], v_stat[:, 8:16], 1.0 / 64, EPS, ALU.mult, ALU.add)\
                    .then_inc(v_var, 1)
                keep(6)
                dve.wait_ge(lin_ready, l + 1)
                for m in range(2):
                    V.tensor_tensor_scan(xc[:, m, :], dec[:, m, :], lin[:, m, :], 0.0, ALU.mult, ALU.add)\
                        .then_inc(h_ready, 1)
                dve.wait_ge(h_ready, l * 2 + 2)
                dve.wait_ge(gate_gelu, l + 1)
                V.tensor_tensor(y_bc[:, 0:2, :], xc[:], gate_z, ALU.mult).then_inc(yb_ready, 1)
                weigh_queries(8)
                step(11)
                keep(7)

                def inverse_bc(c):
                    dve.wait_ge(rms_bc, l * 2 + c + 1)
                    V.reciprocal(inv_bc[:, c], inv_bc[:, c]).then_inc(inv_bc_ready, 1)

                def normalise_bc(c):
                    dve.wait_ge(spread_bc_done, l * 2 + c + 1)
                    for j in range(2):
                        y, gain = y_bc[:, 2 * c + j, :], par[:, C_GBC + 2 * c + j:C_GBC + 2 * c + j + 1]
                        V.scalar_tensor_tensor(y, y, gain, spread_bc_ps[c][:, j, :], ALU.mult, ALU.mult)\
                            .then_inc(nbc_ready, 1)

                def split_bc(c):
                    o = slice(4 + 2 * c, 6 + 2 * c)
                    dve.wait_ge(yhbc, l * 2 + c + 1)
                    V.tensor_tensor(ylo[:, o, :], y_bc[:, 2 * c:2 * c + 2, :], yhi[:, o, :].bitcast(F32), ALU.subtract)\
                        .then_inc(ylbc, 1)

                inverse_bc(0)
                keep(8)
                normalise_bc(0)
                split_bc(0)
                dve.wait_ge(u_gelu, l + 1)
                dve.wait_ge(z_done, l + 1)
                V.tensor_tensor(y_bc[:, 2:4, :], z_ps, u_z, ALU.mult).then_inc(yc_ready, 1)
                lo_mix(l, 13)
                inverse_bc(1)
                dve.wait_ge(osq_ready, l + 1)
                dve.wait_ge(gs_ready, l + 1)
                for h in range(HEADS):
                    ins = V.scalar_tensor_tensor(gz[:, h, :], o_ps[:, h, :], par[:, C_HN + h:C_HN + h + 1],
                                                 gz[:, h, :], ALU.mult, ALU.mult)
                ins.then_inc(og_ready, 1)
                normalise_bc(1)
                split_bc(1)
                dve.wait_ge(rms_a, l + 1)
                V.reciprocal(inv_a[:], inv_a[:]).then_inc(inv_a_ready, 1)
                lo_mix(l, 14)
                dve.wait_ge(og_ready, l + 1)
                for p in range(2):
                    o = slice(2 * p, 2 * p + 2)
                    dve.wait_ge(spread_a_done, l * 2 + p + 1)
                    V.tensor_tensor(gz[:, o, :], spread_a_ps[:, o, :], gz[:, o, :], ALU.mult).then_inc(na_ready, 1)
                for p in range(2):
                    o = slice(2 * p, 2 * p + 2)
                    dve.wait_ge(yha, l * 2 + p + 1)
                    V.tensor_tensor(ylo[:, o, :], gz[:, o, :], yhi[:, o, :].bitcast(F32), ALU.subtract)\
                        .then_inc(yla, 1)
                lo_mix(l, N_MIX - 1)
                lo(ROLES[1][0], use_f(l, 1, ROLES[1][0], 0))

            for slot in range(3):
                dve.sem_inc(lo_ready[slot], 1)
            V.memset(eps_col[:], EPS)
            V.memset(ones_col[:], 1.0).then_inc(ones_made, 1)
            V.memset(xpad[:, :, 0:3], 0.0)
            V.memset(half_ones[0:64, 0:1], 1.0)
            V.memset(half_ones[64:128, 0:1], 0.0)
            V.memset(half_ones[0:64, 1:2], 0.0).then_inc(ones_made, 1)
            V.memset(half_ones[64:128, 1:2], 1.0).then_inc(ones_made, 1)
            dve.wait_ge(par_landed, 16)
            V.tensor_copy(par[:, 0:N_PAR], par_all[:, 0, :]).then_inc(par_ready, 1)
            lo(0, 0)
            dve.wait_ge(par_ready, 1)
            dve.wait_ge(x_landed, 16)
            for m in range(KT):
                split_x(0, C_N1, m)
            with dve.Fori(0, DEPTH) as l:
                lo(1, use_f(l, 0, 1, 0))
                swiglu(l, 0, l * 3)
                residual_and_split(l * 3, l * 3 + 1, C_NM, 0.5)
                lo_mix(l, 1)
                mixer(l, l * 3 + 1)
                residual_and_split(l * 3 + 1, l * 3 + 2, C_N2, 1.0)
                lo(ROLES[1][1], use_f(l, 1, ROLES[1][1], 0))
                swiglu(l, 1, l * 3 + 2)
                V.tensor_copy(par[:, 0:N_PAR], par_all[:, ds(l + 1, 1), :].rearrange("p a c -> p (a c)"))\
                    .then_inc(par_ready, 1)
                dve.wait_ge(par_ready, l + 2)
                residual_and_split(l * 3 + 2, l * 3 + 3, C_N1, 0.5)
            for m in range(KT):
                V.tensor_scalar(xg[m // 4][:, m % 4, :], x[:, m, :], par[:, C_N1 + m:C_N1 + m + 1], None, ALU.mult)\
                    .then_inc(xg_ready, 1)
            dve.wait_ge(xg_ready, KT)
            dve.wait_ge(rps_ready, 3 * DEPTH + 1)
            for b in range(4):
                o = xg[b // 2][:, 2 * (b % 2):2 * (b % 2) + 2, :]
                V.tensor_tensor(o, o, rinv_ps.unsqueeze(1).to_broadcast([P, 2, SEQ]), ALU.mult).then_inc(out_ready, 1)


def chunks_of_columns(w, order=None):
    n = w.shape[1] // CW
    c = w.reshape(KT, P, n, CW).transpose(2, 1, 0, 3).reshape(n, P, CHUNK)
    return c if order is None else c[list(order)]


def chunks_of_rows(w, order=None):
    n = w.shape[0] // (2 * P)
    c = w.reshape(n, 2, P, D).transpose(0, 2, 1, 3).reshape(n, P, CHUNK)
    return c if order is None else c[list(order)]


def swiglu_chunks(wg, wu, wd):
    g, u, d = chunks_of_columns(wg), chunks_of_columns(wu), chunks_of_rows(wd)
    out = [g[0], u[0]]
    for i in range(1, FCH):
        out += [g[i], u[i], d[i - 1]]
    return out + [d[FCH - 1]]


def kernel(**inputs):
    import concourse.bacc as bacc
    from concourse import mybir
    from concourse.bass_utils import run_bass_kernel_spmd

    a = {k: np.asarray(v) for k, v in inputs.items()}
    f32 = np.float32
    stream = np.zeros((DEPTH * PER_LAYER + 1, P, CHUNK), f32)
    at = 0
    for l in range(DEPTH):
        parts = swiglu_chunks(a["ffn1_wg"][l], a["ffn1_wu"][l], a["ffn1_wd"][l])
        parts += list(chunks_of_columns(a["w_in"][l], IN_ORDER)) + list(chunks_of_rows(a["w_out"][l], OUT_ORDER))
        parts += swiglu_chunks(a["ffn2_wg"][l], a["ffn2_wu"][l], a["ffn2_wd"][l])
        for part in parts:
            stream[at] = part
            at += 1

    def tiles(v):
        return v.reshape(-1, P).T

    params = np.zeros((P, DEPTH + 1, N_PAR), f32)
    bd = np.zeros((P, DEPTH, 4, P), f32)
    for l in range(DEPTH):
        for c, v in ((C_N1, a["ffn1_norm"]), (C_NM, a["mix_norm"]), (C_N2, a["ffn2_norm"]), (C_HN, a["hgrn_norm"]),
                     (C_CW, a["conv_w"]), (C_CB, a["conv_b"]), (C_BA, a["lru_ba"]), (C_BX, a["lru_bx"]),
                     (C_LAM, a["lru_lambda"]), (C_GBC, a["lru_norm"]), (C_GBC + 2, a["sgu_norm"]),
                     (C_LBL, a["hgrn_lb_logits"])):
            t = tiles(v[l])
            params[:, l, c:c + t.shape[1]] = t
        for which, w in enumerate((a["lru_wa"], a["lru_wx"])):
            for blk in range(4):
                o = 64 * (blk % 2)
                bd[o:o + 64, l, 2 * which + blk // 2, o:o + 64] = w[l, blk]
    params[:, DEPTH, C_N1:C_N1 + KT] = tiles(a["final_norm"])
    s = np.arange(P)[:, None]
    t = np.arange(P)[None, :]
    masks = []
    for h in HALVES:
        right = t[t % (2 * h) >= h][None, :]
        masks.append((s // (2 * h) == right // (2 * h)) & (s % (2 * h) < h))
    masks = np.concatenate(masks + [s == t], axis=1).astype(f32)
    arrays = {
        "x_t": np.ascontiguousarray(a["x"][0].T.reshape(KT, P, SEQ).transpose(1, 0, 2)),
        "wstream": stream,
        "params": params,
        "block_diag": bd.reshape(P, DEPTH, 4 * P),
        "sgu_wt": np.ascontiguousarray(a["sgu_w"].transpose(3, 0, 1, 2)).reshape(P, DEPTH, 4 * P),
        "sgu_bias": np.tile(a["sgu_b"].transpose(1, 0, 2), (1, 1, TT)),
        "group_rows": (np.arange(4)[:, None] == np.arange(DC)[None, :] // (DC // 4)).astype(f32),
        "identity": np.eye(P, dtype=f32),
        "masks": masks,
        "causal": (s <= t).astype(f32),
    }
    nc = bacc.Bacc("TRN2", target_bir_lowering=False, num_devices=1)
    args = [nc.dram_tensor(k, v.shape, mybir.dt.from_np(v.dtype), kind="ExternalInput").ap()
            for k, v in arrays.items()]
    out = nc.dram_tensor("out_t", (P, KT, SEQ), mybir.dt.float32, kind="ExternalOutput").ap()
    build(nc, *args, out)
    got = run_bass_kernel_spmd(nc, [arrays], core_ids=[0]).results[0]["out_t"]
    return np.ascontiguousarray(got.transpose(1, 0, 2).reshape(D, SEQ).T)[None]
```
